# Optimizing a Trainium2 kernel written in Bass

```python
import jax, jax.numpy as jnp
from jax import lax
import numpy as np

D_MODEL = 1024
BATCH = 1
SEQ = 2048
DEPTH = 1

D_MIX = D_MODEL
D_LRU = D_MIX // 2
LRU_HEADS = 8
LRU_HEAD_DIM = D_LRU // LRU_HEADS
LRU_CONV = 4
LRU_C = 8.0
D_POOL = D_MIX - D_LRU
POOL_WINDOWS = (2, 4, 8, 16)
POOL_GROUPS = len(POOL_WINDOWS)
POOL_GROUP_DIM = D_POOL // POOL_GROUPS
D_IN = 2 * D_LRU + D_POOL
D_FF = 3 * D_MODEL
FFN_CONV = 3
D_PLE = 256
EPS = 1e-6

kernel_name = 'hybrid_rglru_pool_block'

def rms_norm(x, g):
    xf = x.astype(jnp.float32)
    y = xf * lax.rsqrt(jnp.mean(xf * xf, axis=-1, keepdims=True) + EPS)
    return (y * g.astype(jnp.float32)).astype(x.dtype)

def causal_dwconv(x, w, b):
    k, c = w.shape
    y = lax.conv_general_dilated(x, w[:, None, :].astype(x.dtype), window_strides=(1,),
                                 padding=[(k - 1, 0)],
                                 dimension_numbers=('NWC', 'WIO', 'NWC'),
                                 feature_group_count=c)
    return y + b.astype(x.dtype)

def _lin_rec_combine(c1, c2):
    a1, b1 = c1
    a2, b2 = c2
    return a1 * a2, a2 * b1 + b2

def rg_lru(x, w_a, b_a, w_x, b_x, lam):
    bsz, s, _ = x.shape
    xf = x.astype(jnp.float32)
    xh = xf.reshape(bsz, s, LRU_HEADS, LRU_HEAD_DIM)
    r = jax.nn.sigmoid(jnp.einsum('bshi,hij->bshj', xh, w_a.astype(jnp.float32)).reshape(bsz, s, D_LRU) + b_a.astype(jnp.float32))
    i = jax.nn.sigmoid(jnp.einsum('bshi,hij->bshj', xh, w_x.astype(jnp.float32)).reshape(bsz, s, D_LRU) + b_x.astype(jnp.float32))
    log_a = -LRU_C * r * jax.nn.softplus(-lam.astype(jnp.float32))
    a = jnp.exp(log_a)
    mult = jnp.sqrt(-jnp.expm1(2.0 * log_a))
    _, h = lax.associative_scan(_lin_rec_combine, (a, mult * (i * xf)), axis=1)
    return h.astype(x.dtype)

def multiscale_pool(x, w_pool, b_pool, pool_scale):
    bsz, s, _ = x.shape
    xg = x.astype(jnp.float32).reshape(bsz, s, POOL_GROUPS, POOL_GROUP_DIM)
    cs = jnp.cumsum(xg, axis=1)
    count = jnp.arange(1, s + 1, dtype=jnp.float32)[None, :, None]
    outs = []
    for g, w in enumerate(POOL_WINDOWS):
        c = cs[:, :, g]
        lag = jnp.pad(c, ((0, 0), (w, 0), (0, 0)))[:, :s]
        mean = (c - lag) / jnp.minimum(count, float(w))
        outs.append(mean - xg[:, :, g])
    pooled = jnp.stack(outs, axis=2)
    y = jnp.einsum('bsgc,gcd->bsgd', pooled, w_pool.astype(jnp.float32)).reshape(bsz, s, D_POOL)
    y = (y + b_pool.astype(jnp.float32)) * pool_scale.astype(jnp.float32)
    return y.astype(x.dtype)

def setup_inputs(seed: int = 0) -> dict:
    key = jax.random.key(seed)
    ks = jax.random.split(key, 26)
    f32 = jnp.float32

    def nrm(k, shape, fan_in):
        return jax.random.normal(k, shape, f32) * (fan_in ** -0.5)

    def gain(k, shape):
        return 1.0 + 0.05 * jax.random.normal(k, shape, f32)

    def small(k, shape):
        return 0.02 * jax.random.normal(k, shape, f32)

    a_target = jax.random.uniform(ks[9], (DEPTH, D_LRU), f32, 0.9, 0.999)
    base = a_target ** (1.0 / LRU_C)
    lam = jnp.log(base) - jnp.log1p(-base)

    return {
        'x': jax.random.normal(ks[0], (BATCH, SEQ, D_MODEL), f32),
        'p': jax.random.normal(ks[1], (DEPTH, BATCH, SEQ, D_PLE), f32),
        'g_mix': gain(ks[2], (DEPTH, D_MODEL)),
        'w_in': nrm(ks[3], (DEPTH, D_MODEL, D_IN), D_MODEL),
        'w_conv_lru': nrm(ks[4], (DEPTH, LRU_CONV, D_LRU), LRU_CONV),
        'b_conv_lru': small(ks[5], (DEPTH, D_LRU)),
        'w_a': nrm(ks[6], (DEPTH, LRU_HEADS, LRU_HEAD_DIM, LRU_HEAD_DIM), LRU_HEAD_DIM),
        'b_a': small(ks[7], (DEPTH, D_LRU)),
        'w_x': nrm(ks[8], (DEPTH, LRU_HEADS, LRU_HEAD_DIM, LRU_HEAD_DIM), LRU_HEAD_DIM),
        'b_x': small(ks[10], (DEPTH, D_LRU)),
        'lam': lam,
        'w_pool': nrm(ks[11], (DEPTH, POOL_GROUPS, POOL_GROUP_DIM, POOL_GROUP_DIM), POOL_GROUP_DIM),
        'b_pool': small(ks[12], (DEPTH, D_POOL)),
        'pool_scale': gain(ks[13], (DEPTH, D_POOL)),
        'w_out': nrm(ks[14], (DEPTH, D_MIX, D_MODEL), D_MIX),
        'g_ffn': gain(ks[15], (DEPTH, D_MODEL)),
        'w_up': nrm(ks[16], (DEPTH, D_MODEL, 2 * D_FF), D_MODEL),
        'w_conv_ffn': nrm(ks[17], (DEPTH, FFN_CONV, 2 * D_FF), FFN_CONV),
        'b_conv_ffn': small(ks[18], (DEPTH, 2 * D_FF)),
        'w_down': nrm(ks[19], (DEPTH, D_FF, D_MODEL), D_FF),
        'g_ple': gain(ks[20], (DEPTH, D_MODEL)),
        'w_ple_gate': nrm(ks[21], (DEPTH, D_MODEL, D_MODEL), D_MODEL),
        'b_ple_gate': small(ks[22], (DEPTH, D_MODEL)),
        'w_ple_proj': nrm(ks[23], (DEPTH, D_PLE, D_MODEL), D_PLE),
        'g_final': gain(ks[24], (D_MODEL,)),
    }

def reference(x, p, g_mix, w_in, w_conv_lru, b_conv_lru, w_a, b_a, w_x, b_x, lam,
              w_pool, b_pool, pool_scale, w_out, g_ffn, w_up, w_conv_ffn, b_conv_ffn,
              w_down, g_ple, w_ple_gate, b_ple_gate, w_ple_proj, g_final):
    h = x
    for i in range(DEPTH):
        u = rms_norm(h, g_mix[i])
        z = u @ w_in[i]
        z_lru = z[..., :D_LRU]
        z_gate = z[..., D_LRU:2 * D_LRU]
        z_pool = z[..., 2 * D_LRU:]
        xc = causal_dwconv(z_lru, w_conv_lru[i], b_conv_lru[i])
        y_lru = rg_lru(xc, w_a[i], b_a[i], w_x[i], b_x[i], lam[i]) * jax.nn.gelu(z_gate)
        y_pool = multiscale_pool(z_pool, w_pool[i], b_pool[i], pool_scale[i])
        h = h + jnp.concatenate([y_lru, y_pool], axis=-1) @ w_out[i]
        v = rms_norm(h, g_ffn[i])
        up = causal_dwconv(v @ w_up[i], w_conv_ffn[i], b_conv_ffn[i])
        gate = up[..., :D_FF]
        val = up[..., D_FF:]
        h = h + (jax.nn.gelu(gate) * val) @ w_down[i]
        q = rms_norm(h, g_ple[i])
        h = h + jax.nn.sigmoid(q @ w_ple_gate[i] + b_ple_gate[i]) * (p[i] @ w_ple_proj[i])
    return rms_norm(h, g_final)


_drawn_inputs = setup_inputs


def setup_inputs(seed=0):
    import zlib

    import numpy as np

    out = dict(_drawn_inputs(seed))
    spreads = {}
    factors = {'b_a': 36.713,
     'b_x': 28.019,
     'b_pool': 4.837,
     'b_conv_ffn': 4.577,
     'g_ple': 8.0,
     'b_ple_gate': 47.963}
    for name, (base, spread) in spreads.items():
        noise = np.random.default_rng([zlib.crc32(name.encode()), seed]).standard_normal(out[name].shape)
        drawn = base * np.exp(spread * noise) if base else spread * noise
        out[name] = __import__('jax').numpy.asarray(drawn.astype(out[name].dtype))
    for name, factor in factors.items():
        out[name] = (out[name] * factor).astype(out[name].dtype)
    return out
```

```python
from contextlib import ExitStack, contextmanager

import concourse.bass as bass
from concourse import mybir

F32 = mybir.dt.float32
F32R = mybir.dt.float32r
ALU = mybir.AluOpType
ACT = mybir.ActivationFunctionType

P = 128
SEQ, D = 2048, 1024
BLOCK = 1024
BLOCKS = SEQ // BLOCK
BANK = 512
HALVES = BLOCK // BANK
DT = D // P
GROUPS = 4
WINDOWS = (2, 4, 8, 16)
HALO_POOL = 16
LRU_TAPS, FFN_TAPS = 4, 3
HALO_LRU, HALO_FFN = LRU_TAPS - 1, FFN_TAPS - 1
LRU_C = 8.0
EPS = 1e-6
FF = 3 * D
PLE_TILES = 2
CHUNK = 8
CHUNKS = FF // P // CHUNK
KP = 4
PANEL = KP * P
RING = 4
WIDE = BLOCK + HALO_POOL


def plan():
    jobs, panels, ends = {}, {}, []
    used = 0

    def job(name, n_panels):
        nonlocal used
        jobs[name] = len(ends)
        panels[name] = used
        used += n_panels
        ends.append(used)

    def gates(m):
        job(("a", m), 0)
        job(("x", m), 0)
        job(("pool", m), 1)

    job("stat0", 0)
    for m in range(GROUPS):
        job(("L", m), 2)
        if m:
            gates(m - 1)
        job(("G", m), 2)
        job(("P", m), 2)
    gates(GROUPS - 1)
    for m in range(DT):
        job(("out", m), 2)
    job("stat1", 0)
    for c in range(CHUNKS):
        for j in range(CHUNK):
            job(("gate", c, j), 2)
            job(("val", c, j), 2)
        for m in range(DT):
            job(("down", c, m), 2)
    job("stat2", 0)
    for m in range(DT):
        job(("pg", m), 2)
        job(("pp", m), 1)
    job("stat3", 0)
    return jobs, panels, ends


JOBS, PANELS, ENDS = plan()
NJ, NP = len(ENDS), ENDS[-1]
CJ, CP = 3 * CHUNK, 6 * CHUNK
assert NJ % RING == 0 and NP % RING == 0 and CJ % RING == 0 and CP % RING == 0
Y_ORDER = [t for m in range(GROUPS) for t in (GROUPS + m, m)]

COLS = {}


def _cols():
    at = 0
    for name, n in (("g_mix", DT), ("g_ffn", DT), ("g_ple", DT), ("g_final", DT), ("w_lru", LRU_TAPS * GROUPS),
                    ("b_lru", GROUPS), ("b_a", GROUPS), ("b_x", GROUPS), ("lam", GROUPS), ("b_pool", GROUPS),
                    ("pool_scale", GROUPS), ("b_gate", DT), ("ffn", CHUNKS * CHUNK * 2 * (FFN_TAPS + 1))):
        COLS[name] = at
        at += n
    return at


NPAR = _cols()
CHUNK_PAR = CHUNK * 2 * (FFN_TAPS + 1)


class Chain:

    def __init__(self, eng, sem, per_block):
        self.eng, self.sem, self.per_block = eng, sem, per_block
        self.base, self.k = 0, 0

    def mark(self, ins):
        ins.then_inc(self.sem, 1)
        self.k += 1
        return self.base + self.k

    def link(self, ins):
        self.eng.wait_ge(self.sem, self.mark(ins))

    def block(self, b, before):
        self.base, self.k = b * self.per_block + before, 0

    def end(self):
        assert self.k == self.per_block, ("chain per block", self.k)

    @contextmanager
    def loop(self, c, n, per_iter):
        base, k = self.base, self.k
        self.base = base + c * per_iter
        yield
        assert self.k - k == per_iter, ("chain per iteration", self.k - k)
        self.base, self.k = base, k + n * per_iter


def build(nc, xT, pT, wpan, par_d, outT):
    with ExitStack() as ctx:
        def sb(name, shape, dt=F32):
            return ctx.enter_context(nc.sbuf_tensor(name, shape, dt))

        def sem(name):
            return ctx.enter_context(nc.semaphore(name))

        H = sb("H", [P, DT, BLOCK])
        Uhi = sb("Uhi", [P, DT, BLOCK], F32R)
        Ulo = sb("Ulo", [P, DT, BLOCK], F32R)
        Yhi = sb("Yhi", [P, DT, BLOCK], F32R)
        Ylo = sb("Ylo", [P, DT, BLOCK], F32R)
        WG = sb("WG", [P, WIDE])
        WV = sb("WV", [P, WIDE])
        AG = sb("AG", [P, WIDE])
        AV = sb("AV", [P, WIDE])
        RS = sb("RS", [P, BLOCK])
        raw = [sb(f"raw{i}", [P, PANEL]) for i in range(RING)]
        whi = [sb(f"whi{i}", [P, PANEL], F32R) for i in range(RING)]
        wlo = [sb(f"wlo{i}", [P, PANEL], F32R) for i in range(RING)]
        par = sb("par", [P, NPAR])
        cpar_act = sb("cpar_act", [P, CHUNK_PAR])
        cpar_dve = sb("cpar_dve", [P, CHUNK_PAR])
        halo_ffn = sb("halo_ffn", [P, CHUNKS, CHUNK * 2 * HALO_FFN])
        halo_c = sb("halo_c", [P, CHUNK * 2 * HALO_FFN])
        halo_lru = sb("halo_lru", [P, GROUPS * HALO_LRU])
        halo_pool = sb("halo_pool", [P, GROUPS * HALO_POOL])
        ratio = sb("ratio", [P, GROUPS * HALO_POOL])
        state = sb("state", [P, GROUPS])
        means = sb("means", [P, P])
        eps_t = sb("eps_t", [P, 1])
        decay = sb("decay", [P, GROUPS])
        ndecay = sb("ndecay", [P, GROUPS])
        pbs = sb("pbs", [P, GROUPS])
        sp = sb("sp", [P, 5 * GROUPS])

        slot = [ctx.enter_context(nc.psum_tensor(f"slot{i}", [P, BLOCK], F32)) for i in range(RING)]

        X = [H[:, 0, :], H[:, 1, :]]
        G, PO, R, I, S, T = (H[:, k, :] for k in range(2, 8))

        par_in = sem("par_in")
        x_in = [sem(f"x_in{i}") for i in range(4)]
        x_again = [sem(f"x_again{i}") for i in range(4)]
        p_in = sem("p_in")
        panel_in = [sem(f"panel_in{i}") for i in range(RING)]
        panel_hi, panel_lo = sem("panel_hi"), sem("panel_lo")
        jobs_done = sem("jobs_done")
        slot_free = [sem(f"slot_free{i}") for i in range(RING)]
        zeroed = sem("zeroed")
        u_hi, u_ready = sem("u_hi"), sem("u_ready")
        sq_ready, ss_added = sem("sq_ready"), sem("ss_added")
        rms_ready, rstd_ready = sem("rms_ready"), sem("rstd_ready")
        zl_ready, xc_sum, xc_ready = sem("zl_ready"), sem("xc_sum"), sem("xc_ready")
        xh_ready, gates_in = sem("xh_ready"), sem("gates_in")
        tanh_ready, decay_ready, onemin_ready = sem("tanh_ready"), sem("decay_ready"), sem("onemin_ready")
        mult_ready, gelu_ready = sem("mult_ready"), sem("gelu_ready")
        y_raw, y_hi, y_ready = sem("y_raw"), sem("y_hi"), sem("y_ready")
        pooled_raw, pooled_hi, pool_in = sem("pooled_raw"), sem("pooled_hi"), sem("pool_in")
        ug_ready, uv_ready = sem("ug_ready"), sem("uv_ready")
        g_sum, v_sum, g_conv, g_act = sem("g_sum"), sem("v_sum"), sem("g_conv"), sem("g_act")
        f_raw, f_hi, f_ready = sem("f_raw"), sem("f_hi"), sem("f_ready")
        p_hi, p_ready = sem("p_hi"), sem("p_ready")
        sg_ready, h_done = sem("sg_ready"), sem("h_done")
        out_ready = sem("out_ready")
        out_written = [sem(f"out_written{i}") for i in range(4)]
        dve_chain, act_chain = sem("dve_chain"), sem("act_chain")
        sp_dve, sp_act = sem("sp_dve"), sem("sp_act")

        def col(name, i):
            return par[:, COLS[name] + i:COLS[name] + i + 1]

        def taps(tile, j, stream, t):
            i = (2 * j + stream) * (FFN_TAPS + 1) + t
            return tile[:, i:i + 1]

        def job_count(b, j):
            return b * NJ + j + 1

        def free_count(b, j):
            return b * (NJ // RING) + j // RING + 1

        x_tiles = xT.rearrange("(k p) (b t) -> b p k t", p=P, t=BLOCK)
        p_tiles = pT.rearrange("(k p) (b t) -> b p k t", p=P, t=BLOCK)
        out_tiles = outT.rearrange("(k p) (b t) -> b p k t", p=P, t=BLOCK)
        panel_groups = wpan.rearrange("(g s) p c -> g s p c", s=RING)
        GROUPS_OF_PANELS = NP // RING

        block = ctx.enter_context(nc.Block())

        @block.sync
        def _(sync):
            def x_load(b, sems):
                for q in range(4):
                    sync.dma_start(H[:, 2 * q:2 * q + 2, :], x_tiles[b, :, 2 * q:2 * q + 2, :]
                                   ).then_inc(sems[q], 16)

            def panel_group(b, g, static_g=None):
                for s in range(RING):
                    sync.wait_ge(panel_lo, (b * GROUPS_OF_PANELS + g) * RING + (s + 1 - RING))
                    sync.dma_start(raw[s][:], panel_groups[g if static_g is None else static_g, s]
                                   ).then_inc(panel_in[s], 16)

            sync.dma_start(par[:], par_d).then_inc(par_in, 16)
            for s in range(RING):
                sync.dma_start(raw[s][:], panel_groups[0, s]).then_inc(panel_in[s], 16)
            with sync.Fori(0, BLOCKS) as b:
                for q in range(4):
                    sync.wait_ge(out_written[q], b * 16 + 16)
                    sync.dma_start(H[:, 2 * q:2 * q + 2, :], x_tiles[b, :, 2 * q:2 * q + 2, :]
                                   ).then_inc(x_in[q], 16)
                mix_groups = PANELS[("out", 0)] // RING
                with sync.Fori(1, mix_groups + 1) as g:
                    panel_group(b, g)
                sync.wait_ge(y_ready, b * DT + DT)
                x_load(b, x_again)
                ffn_groups = PANELS["stat2"] // RING
                with sync.Fori(mix_groups + 1, ffn_groups) as g:
                    panel_group(b, g)
                sync.wait_ge(f_ready, b * (CHUNKS * CHUNK) + CHUNKS * CHUNK)
                for k, tile in enumerate((WG, WV)):
                    sync.dma_start(tile[:, 0:BLOCK], p_tiles[b, :, k, :]).then_inc(p_in, 16)
                with sync.Fori(ffn_groups, GROUPS_OF_PANELS) as g:
                    panel_group(b, g)
                panel_group(b, GROUPS_OF_PANELS, 0)
                for q in range(4):
                    sync.wait_ge(out_ready, b * DT + 2 * q + 2)
                    sync.dma_start(out_tiles[b, :, 2 * q:2 * q + 2, :], H[:, 2 * q:2 * q + 2, :]
                                   ).then_inc(out_written[q], 16)
            for q in range(4):
                sync.wait_ge(out_written[q], BLOCKS * 16 + 16)

        @block.gpsimd
        def _(pool):
            for q in range(4):
                pool.sem_inc(out_written[q], 16)

        @block.tensor
        def _(pe):
            def panel_products(b_panels, n, j, rhs, k0, ks, first, last, ready=None):
                ps = slot[j % RING]
                pe.wait_ge(panel_lo, b_panels + n + 1)
                for k in range(ks):
                    if ready is not None:
                        pe.wait_ge(*ready(k0 + k))
                    w = slice(k * P, (k + 1) * P)
                    hi, lo = rhs(k0 + k)
                    passes = ((whi, hi), (whi, lo), (wlo, hi))
                    for i, (stat, mov) in enumerate(passes):
                        for h in range(HALVES):
                            t = slice(h * BANK, (h + 1) * BANK)
                            mm = pe.matmul(ps[:, t], stat[n % RING][:, w], mov[:, t],
                                           start=first and k == 0 and i == 0,
                                           stop=last and k == ks - 1 and i == len(passes) - 1)
                return mm

            def projection(b, j, n, rhs, tiles, ready=None, at=0, block_jobs=None, block_panels=None):
                pe.wait_ge(slot_free[j % RING], (b * (NJ // RING) if block_jobs is None else block_jobs) + j // RING + 1)
                bp = b * NP if block_panels is None else block_panels
                for i in range(0, tiles, KP):
                    mm = panel_products(bp, n + i // KP, j, rhs, i, min(KP, tiles - i),
                                        i == 0, i + KP >= tiles, ready)
                mm.then_inc(jobs_done, 1)

            def u(k):
                return Uhi[:, k, :], Ulo[:, k, :]

            def y(k):
                return Yhi[:, k, :], Ylo[:, k, :]

            def stat(b, n):
                j = JOBS[f"stat{n}"]
                pe.wait_ge(ss_added, b * (4 * (DT - 1)) + (n + 1) * (DT - 1))
                pe.wait_ge(slot_free[j % RING], free_count(b, j))
                for h in range(HALVES):
                    t = slice(h * BANK, (h + 1) * BANK)
                    mm = pe.matmul(slot[j % RING][:, t], means[:], AV[:, t], start=True, stop=True)
                mm.then_inc(jobs_done, 1)

            def gates(b, m):
                n = PANELS[("pool", m)]
                pe.wait_ge(panel_lo, b * NP + n + 1)
                for i, (name, tile, ready) in enumerate((("a", 2 * m + 1, gates_in), ("x", 2 * m + 1, gates_in),
                                                         ("pool", 2 * m, pool_in))):
                    j = JOBS[(name, m)]
                    pe.wait_ge(ready, b * GROUPS + m + 1)
                    pe.wait_ge(slot_free[j % RING], free_count(b, j))
                    hi, lo = y(tile)
                    w = slice(i * P, (i + 1) * P)
                    passes = ((whi, hi), (whi, lo), (wlo, hi))
                    for q, (stat_, mov) in enumerate(passes):
                        for h in range(HALVES):
                            t = slice(h * BANK, (h + 1) * BANK)
                            mm = pe.matmul(slot[j % RING][:, t], stat_[n % RING][:, w], mov[:, t],
                                           start=q == 0, stop=q == 2)
                    mm.then_inc(jobs_done, 1)

            def after_norm(b, n):
                return lambda k: (u_ready, b * (3 * DT) + n * DT + k + 1)

            pe.wait_ge(zeroed, 1)
            with pe.Fori(0, BLOCKS) as b:
                stat(b, 0)
                for m in range(GROUPS):
                    for name in ("L", "G", "P"):
                        projection(b, JOBS[(name, m)], PANELS[(name, m)], u, DT,
                                   after_norm(b, 0) if (name, m) == ("L", 0) else None)
                        if name == "L" and m:
                            gates(b, m - 1)
                gates(b, GROUPS - 1)
                for m in range(DT):
                    projection(b, JOBS[("out", m)], PANELS[("out", m)], y, DT,
                               (lambda k: (y_ready, b * DT + k + 1)) if m == 0 else None)
                stat(b, 1)
                with pe.Fori(0, CHUNKS) as c:
                    jb = b * (NJ // RING) + c * (CJ // RING)
                    pb = b * NP + c * CP
                    for j in range(CHUNK):
                        for name in ("gate", "val"):
                            projection(b, JOBS[(name, 0, j)], PANELS[(name, 0, j)], u, DT,
                                       after_norm(b, 1) if (name, j) == ("gate", 0) else None,
                                       block_jobs=jb, block_panels=pb)
                    for m in range(DT):
                        projection(b, JOBS[("down", 0, m)], PANELS[("down", 0, m)], y, CHUNK,
                                   (lambda k: (f_ready, b * (CHUNKS * CHUNK) + c * CHUNK + k + 1)) if m == 0 else None,
                                   block_jobs=jb, block_panels=pb)
                stat(b, 2)
                for m in range(DT):
                    projection(b, JOBS[("pg", m)], PANELS[("pg", m)], u, DT, after_norm(b, 2) if m == 0 else None)
                    projection(b, JOBS[("pp", m)], PANELS[("pp", m)], y, PLE_TILES,
                               (lambda k: (p_ready, b * PLE_TILES + k + 1)) if m == 0 else None)
                stat(b, 3)

        @block.scalar
        def _(act):
            def split(b, first, last, after=None, base=None):
                bp, bg, bj = base or (b * NP, b * (NP // RING), b * NJ)
                if after is not None and last > first:
                    act.wait_ge(jobs_done, bj + after + 1)
                for n in range(first, last):
                    act.wait_ge(panel_in[n % RING], (bg + n // RING) * 16 + 16)
                    nc.scalar.activation(whi[n % RING][:], raw[n % RING][:], ACT.Copy).then_inc(panel_hi, 1)

            def refill(b, j, base=None):
                split(b, (ENDS[j - 1] if j else 0) + RING, ENDS[j] + RING, j, base)

            def norm_tile(b, n, m, g, ready=()):
                for w in ready:
                    act.wait_ge(*w)
                if g is not None:
                    nc.scalar.activation(Uhi[:, m, :], H[:, m, :], ACT.Copy, scale=g).then_inc(u_hi, 1)
                if m >= 2:
                    act.wait_ge(ss_added, b * (4 * (DT - 1)) + n * (DT - 1) + m - 1)
                nc.scalar.activation((AG if m else AV)[:, 0:BLOCK], H[:, m, :], ACT.Square).then_inc(sq_ready, 1)

            def rms(b, n):
                j = JOBS[f"stat{n}"]
                act.wait_ge(jobs_done, job_count(b, j))
                nc.scalar.activation(RS[:], slot[j % RING][:], ACT.Sqrt, bias=eps_t[:]).then_inc(rms_ready, 1)

            act.wait_ge(par_in, 16)
            lam = par[:, COLS["lam"]:COLS["lam"] + GROUPS]
            nc.scalar.activation(sp[:, 0:GROUPS], lam, ACT.Abs).then_inc(sp_act, 1)
            act.wait_ge(sp_act, 1)
            nc.scalar.activation(sp[:, 0:GROUPS], sp[:, 0:GROUPS], ACT.Exp, scale=-1.0).then_inc(sp_act, 1)
            split(0, 0, RING)
            act.wait_ge(zeroed, 1)
            act.wait_ge(sp_dve, 1)

            with act.Fori(0, BLOCKS) as b:
                for m in range(DT):
                    norm_tile(b, 0, m, col("g_mix", m),
                              [(x_in[m // 2], b * 16 + 16)] if m % 2 == 0 else [])
                rms(b, 0)

                def recurrence_input(m):
                    j = JOBS[("L", m)]
                    refill(b, j)
                    act.wait_ge(zl_ready, b * GROUPS + m + 1)
                    nc.scalar.activation(X[m % 2], WG[:, HALO_LRU:HALO_LRU + BLOCK], ACT.Identity,
                                         bias=col("b_lru", m), scale=col("w_lru", 4 * m + 3)).then_inc(xc_sum, 1)
                    act.wait_ge(xc_ready, b * GROUPS + m + 1)
                    nc.scalar.activation(Yhi[:, 2 * m + 1, :], X[m % 2], ACT.Copy).then_inc(xh_ready, 1)

                def recurrence(m):
                    ja, jx, jp = (JOBS[(n, m)] for n in ("a", "x", "pool"))
                    act.wait_ge(jobs_done, job_count(b, ja))
                    nc.scalar.activation(R, slot[ja % RING][:], ACT.Sigmoid, bias=col("b_a", m)
                                         ).then_inc(slot_free[ja % RING], 1)
                    act.wait_ge(jobs_done, job_count(b, jx))
                    nc.scalar.activation(I, slot[jx % RING][:], ACT.Sigmoid, bias=col("b_x", m)
                                         ).then_inc(slot_free[jx % RING], 1)
                    act.wait_ge(slot_free[ja % RING], free_count(b, ja) + 1)
                    nc.scalar.activation(S, R, ACT.Tanh, scale=decay[:, m:m + 1]).then_inc(tanh_ready, 1)
                    nc.scalar.activation(R, R, ACT.Exp, scale=ndecay[:, m:m + 1]).then_inc(decay_ready, 1)
                    act.wait_ge(jobs_done, job_count(b, jp))
                    nc.scalar.activation(PO, slot[jp % RING][:], ACT.Identity, bias=pbs[:, m:m + 1],
                                         scale=col("pool_scale", m)).then_inc(slot_free[jp % RING], 1)
                    act.wait_ge(slot_free[jp % RING], free_count(b, jp) + 1)
                    nc.scalar.activation(Yhi[:, 2 * m, :], PO, ACT.Copy).then_inc(y_hi, 1)
                    refill(b, jp)
                    act.wait_ge(onemin_ready, b * GROUPS + m + 1)
                    nc.scalar.activation(S, S, ACT.Sqrt, scale=2.0).then_inc(mult_ready, 1)
                    act.wait_ge(y_raw, b * GROUPS + m + 1)
                    nc.scalar.activation(Yhi[:, 2 * m + 1, :], S, ACT.Copy).then_inc(y_hi, 1)

                def gate_and_pool(m):
                    jg, jp = JOBS[("G", m)], JOBS[("P", m)]
                    refill(b, jg)
                    act.wait_ge(slot_free[jg % RING], free_count(b, jg) + 1)
                    nc.scalar.activation(G, G, ACT.Gelu_apprx_tanh).then_inc(gelu_ready, 1)
                    refill(b, jp)
                    act.wait_ge(pooled_raw, b * GROUPS + m + 1)
                    src = AV if m % 2 == 0 else AG
                    nc.scalar.activation(Yhi[:, 2 * m, :], src[:, HALO_POOL:WIDE], ACT.Copy).then_inc(pooled_hi, 1)

                for m in range(GROUPS + 1):
                    if m < GROUPS:
                        recurrence_input(m)
                    if m:
                        recurrence(m - 1)
                    if m < GROUPS:
                        gate_and_pool(m)

                for m in range(DT):
                    j = JOBS[("out", m)]
                    refill(b, j)
                    norm_tile(b, 1, m, col("g_ffn", m), [(slot_free[j % RING], free_count(b, j) + 1)])
                rms(b, 1)

                def chunk(c, last):
                    base = (b * NP + c * CP, b * (NP // RING) + c * (CP // RING), b * NJ + c * CJ)
                    pairs = b * (CHUNKS * CHUNK) + c * CHUNK
                    at = c * CHUNK_PAR + COLS["ffn"]
                    nc.scalar.copy(cpar_act[:], par[:, bass.ds(at, CHUNK_PAR)]).then_inc(act_chain, 1)
                    act.wait_ge(act_chain, b * CHUNKS + c + 1)
                    for j in range(CHUNK):
                        refill(b, JOBS[("gate", 0, j)], base)
                        act.wait_ge(ug_ready, pairs + j + 1)
                        nc.scalar.activation(AG[:, 0:BLOCK], WG[:, HALO_FFN:HALO_FFN + BLOCK], ACT.Identity,
                                             bias=taps(cpar_act, j, 0, 3), scale=taps(cpar_act, j, 0, 2)
                                             ).then_inc(g_sum, 1)
                        act.wait_ge(g_conv, pairs + j + 1)
                        nc.scalar.activation(AG[:, 0:BLOCK], AG[:, 0:BLOCK], ACT.Gelu_apprx_tanh).then_inc(g_act, 1)
                        refill(b, JOBS[("val", 0, j)], base)
                        act.wait_ge(uv_ready, pairs + j + 1)
                        nc.scalar.activation(AV[:, 0:BLOCK], WV[:, HALO_FFN:HALO_FFN + BLOCK], ACT.Identity,
                                             bias=taps(cpar_act, j, 1, 3), scale=taps(cpar_act, j, 1, 2)
                                             ).then_inc(v_sum, 1)
                        act.wait_ge(f_raw, pairs + j + 1)
                        nc.scalar.activation(Yhi[:, j, :], AV[:, 0:BLOCK], ACT.Copy).then_inc(f_hi, 1)
                    for m in range(DT):
                        j = JOBS[("down", 0, m)]
                        refill(b, j, base)
                        if last:
                            jl = JOBS[("down", c, m)]
                            norm_tile(b, 2, m, col("g_ple", m), [(slot_free[jl % RING], free_count(b, jl) + 1)])

                with act.Fori(0, CHUNKS - 1) as c:
                    chunk(c, False)
                chunk(CHUNKS - 1, True)
                for k, tile in enumerate((WG, WV)):
                    if k == 0:
                        act.wait_ge(jobs_done, job_count(b, JOBS[("down", CHUNKS - 1, DT - 1)]))
                        act.wait_ge(p_in, b * 32 + 32)
                    nc.scalar.activation(Yhi[:, k, :], tile[:, 0:BLOCK], ACT.Copy).then_inc(p_hi, 1)
                rms(b, 2)
                for m in range(DT):
                    jg, jp = JOBS[("pg", m)], JOBS[("pp", m)]
                    refill(b, jg)
                    act.wait_ge(slot_free[jg % RING], free_count(b, jg) + 1)
                    nc.scalar.activation(WG[:, 0:BLOCK], WG[:, 0:BLOCK], ACT.Sigmoid, bias=col("b_gate", m)
                                         ).then_inc(sg_ready, 1)
                    refill(b, jp)
                    norm_tile(b, 3, m, None, [(h_done, b * DT + m + 1)])
                rms(b, 3)

        @block.vector
        def _(dve):
            v = nc.vector
            chain = Chain(dve, dve_chain, DVE_PER_BLOCK)

            def f32(ap):
                return ap.bitcast(F32)

            def split(first, last, bp):
                for n in range(first, last):
                    dve.wait_ge(panel_hi, bp + n + 1)
                    v.tensor_tensor(wlo[n % RING][:], raw[n % RING][:], f32(whi[n % RING][:]), ALU.subtract
                                    ).then_inc(panel_lo, 1)

            def refill(j, bp):
                split((ENDS[j - 1] if j else 0) + RING, ENDS[j] + RING, bp)

            def scaled_out(b, j, dst, bj=None, bs=None):
                dve.wait_ge(jobs_done, (b * NJ if bj is None else bj) + j + 1)
                v.tensor_tensor(dst, slot[j % RING][:], RS[:], ALU.mult).then_inc(slot_free[j % RING], 1)
                dve.wait_ge(slot_free[j % RING], (b * (NJ // RING) if bs is None else bs) + j // RING + 2)

            def norm_tile(b, n, m, g):
                if g is not None:
                    dve.wait_ge(u_hi, b * (3 * DT) + n * DT + m + 1)
                    v.scalar_tensor_tensor(Ulo[:, m, :], H[:, m, :], g, f32(Uhi[:, m, :]), ALU.mult, ALU.subtract
                                           ).then_inc(u_ready, 1)
                if m:
                    dve.wait_ge(sq_ready, b * (4 * DT) + n * DT + m + 1)
                    if m >= 2:
                        dve.wait_ge(ss_added, b * (4 * (DT - 1)) + n * (DT - 1) + m - 1)
                    v.tensor_tensor(AV[:, 0:BLOCK], AV[:, 0:BLOCK], AG[:, 0:BLOCK], ALU.add).then_inc(ss_added, 1)

            def rstd(b, n):
                j = JOBS[f"stat{n}"]
                t = AV[:, 0:BLOCK]
                dve.wait_ge(rms_ready, b * 4 + n + 1)
                chain.link(v.reciprocal(RS[:], RS[:]))
                chain.link(v.tensor_tensor(t, RS[:], RS[:], ALU.mult))
                v.scalar_tensor_tensor(t, slot[j % RING][:], eps_t[:], t, ALU.add, ALU.mult
                                       ).then_inc(slot_free[j % RING], 1)
                dve.wait_ge(slot_free[j % RING], free_count(b, j) + 1)
                chain.link(v.tensor_scalar(t, t, -0.5, 1.5, ALU.mult, ALU.add))
                return chain.mark(v.tensor_tensor(RS[:], RS[:], t, ALU.mult))

            chain.link(v.memset(means[:], 1.0 / D))
            chain.link(v.memset(eps_t[:], EPS))
            chain.link(v.memset(halo_ffn[:], 0.0))
            chain.link(v.memset(halo_lru[:], 0.0))
            chain.link(v.memset(halo_pool[:], 0.0))
            chain.link(v.memset(state[:], 0.0))
            chain.link(v.memset(ratio[:], 1.0))
            for g, w in enumerate(WINDOWS):
                for t in range(w - 1):
                    chain.link(v.memset(ratio[:, g * HALO_POOL + t:g * HALO_POOL + t + 1], w / (t + 1.0)))
            dve.sem_inc(zeroed, 1)
            for s in range(RING):
                dve.sem_inc(slot_free[s], 1)
            e, z, z2, q, neg = (sp[:, i * GROUPS:(i + 1) * GROUPS] for i in range(5))
            lam = par[:, COLS["lam"]:COLS["lam"] + GROUPS]
            dve.wait_ge(zeroed, 1)
            dve.wait_ge(sp_act, 2)
            chain.link(v.tensor_scalar(z, e, 2.0, None, ALU.add))
            chain.link(v.reciprocal(z, z))
            chain.link(v.tensor_tensor(z, z, e, ALU.mult))
            chain.link(v.tensor_tensor(z2, z, z, ALU.mult))
            chain.link(v.tensor_scalar(q, z2, 1.0 / 17, None, ALU.mult))
            for d in (15, 13, 11, 9, 7, 5, 3):
                chain.link(v.scalar_tensor_tensor(q, q, 1.0 / d, z2, ALU.add, ALU.mult))
            chain.link(v.scalar_tensor_tensor(q, q, 1.0, z, ALU.add, ALU.mult))
            chain.link(v.tensor_scalar(q, q, 2.0, None, ALU.mult))
            chain.link(v.tensor_scalar(neg, lam, -1.0, 0.0, ALU.mult, ALU.max))
            chain.link(v.tensor_tensor(q, q, neg, ALU.add))
            chain.link(v.tensor_scalar(decay[:], q, LRU_C, None, ALU.mult))
            chain.link(v.tensor_scalar(ndecay[:], q, -LRU_C, None, ALU.mult))
            v.tensor_tensor(pbs[:], par[:, COLS["b_pool"]:COLS["b_pool"] + GROUPS],
                            par[:, COLS["pool_scale"]:COLS["pool_scale"] + GROUPS], ALU.mult).then_inc(sp_dve, 1)
            split(0, RING, 0)
            before = chain.k

            with dve.Fori(0, BLOCKS) as b:
                chain.block(b, before)
                bp = b * NP
                for m in range(DT):
                    norm_tile(b, 0, m, col("g_mix", m))
                dve.wait_ge(dve_chain, rstd(b, 0))

                def recurrence_input(m):
                    j = JOBS[("L", m)]
                    halo = halo_lru[:, m * HALO_LRU:(m + 1) * HALO_LRU]
                    v.tensor_copy(WG[:, 0:HALO_LRU], halo)
                    scaled_out(b, j, WG[:, HALO_LRU:HALO_LRU + BLOCK])
                    v.tensor_copy(halo, WG[:, BLOCK:BLOCK + HALO_LRU]).then_inc(zl_ready, 1)
                    refill(j, bp)
                    dve.wait_ge(xc_sum, b * GROUPS + m + 1)
                    for t in (2, 1, 0):
                        tap = v.scalar_tensor_tensor(X[m % 2], WG[:, t:t + BLOCK], col("w_lru", 4 * m + t), X[m % 2],
                                                     ALU.mult, ALU.add)
                        if t:
                            chain.link(tap)
                        else:
                            tap.then_inc(xc_ready, 1)
                    dve.wait_ge(xh_ready, b * GROUPS + m + 1)
                    v.tensor_tensor(Ylo[:, 2 * m + 1, :], X[m % 2], f32(Yhi[:, 2 * m + 1, :]), ALU.subtract
                                    ).then_inc(gates_in, 1)

                def recurrence(m):
                    jx, jp = JOBS[("x", m)], JOBS[("pool", m)]
                    dve.wait_ge(tanh_ready, b * GROUPS + m + 1)
                    chain.link(v.tensor_scalar(T, S, 1.0, None, ALU.add))
                    chain.link(v.reciprocal(T, T))
                    v.tensor_tensor(S, S, T, ALU.mult).then_inc(onemin_ready, 1)
                    dve.wait_ge(slot_free[jx % RING], free_count(b, jx) + 1)
                    input_gated = chain.mark(v.tensor_tensor(I, I, X[m % 2], ALU.mult))
                    dve.wait_ge(y_hi, b * DT + 2 * m + 1)
                    v.tensor_tensor(Ylo[:, 2 * m, :], PO, f32(Yhi[:, 2 * m, :]), ALU.subtract).then_inc(y_ready, 1)
                    refill(jp, bp)
                    dve.wait_ge(dve_chain, input_gated)
                    dve.wait_ge(mult_ready, b * GROUPS + m + 1)
                    chain.link(v.tensor_tensor(I, I, S, ALU.mult))
                    dve.wait_ge(decay_ready, b * GROUPS + m + 1)
                    chain.link(v.tensor_tensor_scan(S, R, I, state[:, m:m + 1], ALU.mult, ALU.add))
                    chain.link(v.tensor_copy(state[:, m:m + 1], S[:, BLOCK - 1:BLOCK]))
                    dve.wait_ge(gelu_ready, b * GROUPS + m + 1)
                    v.tensor_tensor(S, S, G, ALU.mult).then_inc(y_raw, 1)
                    dve.wait_ge(y_hi, b * DT + 2 * m + 2)
                    v.tensor_tensor(Ylo[:, 2 * m + 1, :], S, f32(Yhi[:, 2 * m + 1, :]), ALU.subtract
                                    ).then_inc(y_ready, 1)

                def gate_and_pool(m):
                    jg, jp = JOBS[("G", m)], JOBS[("P", m)]
                    scaled_out(b, jg, G)
                    refill(jg, bp)
                    halo = halo_pool[:, m * HALO_POOL:(m + 1) * HALO_POOL]
                    v.tensor_copy(WV[:, 0:HALO_POOL], halo)
                    scaled_out(b, jp, WV[:, HALO_POOL:WIDE])
                    chain.link(v.tensor_copy(halo, WV[:, BLOCK:WIDE]))
                    src, dst, w = WV, AG, 1
                    while w < WINDOWS[m]:
                        chain.link(v.tensor_tensor(dst[:, 2 * w:WIDE], src[:, 2 * w:WIDE], src[:, w:WIDE - w], ALU.add))
                        src, dst, w = dst, (AV if dst is AG else AG), 2 * w
                    chain.link(v.tensor_tensor(src[:, HALO_POOL:2 * HALO_POOL], src[:, HALO_POOL:2 * HALO_POOL],
                                               ratio[:, m * HALO_POOL:(m + 1) * HALO_POOL], ALU.mult))
                    v.scalar_tensor_tensor(dst[:, HALO_POOL:WIDE], src[:, HALO_POOL:WIDE], 1.0 / w,
                                           WV[:, HALO_POOL:WIDE], ALU.mult, ALU.subtract).then_inc(pooled_raw, 1)
                    refill(jp, bp)
                    dve.wait_ge(pooled_hi, b * GROUPS + m + 1)
                    v.tensor_tensor(Ylo[:, 2 * m, :], dst[:, HALO_POOL:WIDE], f32(Yhi[:, 2 * m, :]), ALU.subtract
                                    ).then_inc(pool_in, 1)

                for m in range(GROUPS + 1):
                    if m < GROUPS:
                        recurrence_input(m)
                    if m:
                        recurrence(m - 1)
                    if m < GROUPS:
                        gate_and_pool(m)
                v.memset(ratio[:], 1.0)

                for m in range(DT):
                    j = JOBS[("out", m)]
                    dve.wait_ge(jobs_done, job_count(b, j))
                    if m % 2 == 0:
                        dve.wait_ge(x_again[m // 2], b * 16 + 16)
                    v.tensor_tensor(H[:, m, :], slot[j % RING][:], H[:, m, :], ALU.add
                                    ).then_inc(slot_free[j % RING], 1)
                    refill(j, bp)
                    norm_tile(b, 1, m, col("g_ffn", m))
                ffn_scale = rstd(b, 1)

                def chunk(c, last):
                    bp_c, bj, bs = b * NP + c * CP, b * NJ + c * CJ, b * (NJ // RING) + c * (CJ // RING)
                    pairs = b * (CHUNKS * CHUNK) + c * CHUNK
                    v.tensor_copy(cpar_dve[:], par[:, bass.ds(c * CHUNK_PAR + COLS["ffn"], CHUNK_PAR)])
                    chain.link(v.tensor_copy(halo_c[:], halo_ffn[:, bass.ds(c, 1), :]))

                    def f_lo(j):
                        dve.wait_ge(f_hi, pairs + j + 1)
                        v.tensor_tensor(Ylo[:, j, :], AV[:, 0:BLOCK], f32(Yhi[:, j, :]), ALU.subtract
                                        ).then_inc(f_ready, 1)

                    def conv(j, stream, work, acc, ready, summed):
                        jj = JOBS[(("gate", "val")[stream], 0, j)]
                        i = (2 * j + stream) * HALO_FFN
                        v.tensor_copy(work[:, 0:HALO_FFN], halo_c[:, i:i + HALO_FFN])
                        if (j, stream) == (0, 0):
                            dve.wait_ge(dve_chain, ffn_scale)
                        scaled_out(b, jj, work[:, HALO_FFN:HALO_FFN + BLOCK], bj, bs)
                        if stream == 0 and j:
                            f_lo(j - 1)
                        v.tensor_copy(halo_c[:, i:i + HALO_FFN], work[:, BLOCK:BLOCK + HALO_FFN]).then_inc(ready, 1)
                        refill(jj, bp_c)
                        dve.wait_ge(summed, pairs + j + 1)
                        chain.link(v.scalar_tensor_tensor(acc[:, 0:BLOCK], work[:, 1:1 + BLOCK],
                                                          taps(cpar_dve, j, stream, 1), acc[:, 0:BLOCK],
                                                          ALU.mult, ALU.add))
                        return v.scalar_tensor_tensor(acc[:, 0:BLOCK], work[:, 0:BLOCK],
                                                      taps(cpar_dve, j, stream, 0), acc[:, 0:BLOCK],
                                                      ALU.mult, ALU.add)

                    for j in range(CHUNK):
                        conv(j, 0, WG, AG, ug_ready, g_sum).then_inc(g_conv, 1)
                        chain.link(conv(j, 1, WV, AV, uv_ready, v_sum))
                        dve.wait_ge(g_act, pairs + j + 1)
                        v.tensor_tensor(AV[:, 0:BLOCK], AG[:, 0:BLOCK], AV[:, 0:BLOCK], ALU.mult).then_inc(f_raw, 1)
                    f_lo(CHUNK - 1)
                    v.tensor_copy(halo_ffn[:, bass.ds(c, 1), :], halo_c[:])
                    for m in range(DT):
                        jj = JOBS[("down", 0, m)]
                        dve.wait_ge(jobs_done, bj + jj + 1)
                        v.tensor_tensor(H[:, m, :], slot[jj % RING][:], H[:, m, :], ALU.add
                                        ).then_inc(slot_free[jj % RING], 1)
                        refill(jj, bp_c)
                        if last:
                            norm_tile(b, 2, m, col("g_ple", m))

                with dve.Fori(0, CHUNKS - 1) as c, chain.loop(c, CHUNKS - 1, DVE_PER_CHUNK):
                    chunk(c, False)
                chunk(CHUNKS - 1, True)
                for k, tile in enumerate((WG, WV)):
                    dve.wait_ge(p_hi, b * PLE_TILES + k + 1)
                    v.tensor_tensor(Ylo[:, k, :], tile[:, 0:BLOCK], f32(Yhi[:, k, :]), ALU.subtract
                                    ).then_inc(p_ready, 1)
                dve.wait_ge(dve_chain, rstd(b, 2))
                for m in range(DT):
                    jg, jp = JOBS[("pg", m)], JOBS[("pp", m)]
                    scaled_out(b, jg, WG[:, 0:BLOCK])
                    refill(jg, bp)
                    dve.wait_ge(sg_ready, b * DT + m + 1)
                    dve.wait_ge(jobs_done, job_count(b, jp))
                    v.tensor_tensor(WV[:, 0:BLOCK], slot[jp % RING][:], WG[:, 0:BLOCK], ALU.mult
                                    ).then_inc(slot_free[jp % RING], 1)
                    refill(jp, bp)
                    dve.wait_ge(slot_free[jp % RING], free_count(b, jp) + 1)
                    v.tensor_tensor(H[:, m, :], H[:, m, :], WV[:, 0:BLOCK], ALU.add).then_inc(h_done, 1)
                    norm_tile(b, 3, m, None)
                dve.wait_ge(dve_chain, rstd(b, 3))
                for m in range(DT):
                    v.scalar_tensor_tensor(H[:, m, :], H[:, m, :], col("g_final", m), RS[:], ALU.mult, ALU.mult
                                           ).then_inc(out_ready, 1)
                chain.end()


DVE_PER_BLOCK = 141
DVE_PER_CHUNK = 25


def pack_panels(i):
    import numpy as np
    w_in, w_out, w_up, w_down, w_gate, w_proj = (
        np.asarray(i[n])[0].reshape(-1, P, np.asarray(i[n]).shape[-1])
        for n in ("w_in", "w_out", "w_up", "w_down", "w_ple_gate", "w_ple_proj"))
    w_a, w_x, w_pool = (np.asarray(i[n])[0] for n in ("w_a", "w_x", "w_pool"))
    out = np.zeros((NP, P, KP, P), w_in.dtype)

    def put(first, w, tiles, m):
        for n, k in enumerate(tiles):
            out[first + n // KP, :, n % KP, :] = w[k, :, m * P:(m + 1) * P]

    for m in range(GROUPS):
        for s, name in enumerate(("L", "G", "P")):
            put(PANELS[(name, m)], w_in, range(DT), s * GROUPS + m)
        n = PANELS[("pool", m)]
        d = w_a.shape[-1]
        for e in range(P // d):
            rows = slice(e * d, (e + 1) * d)
            out[n, rows, 0, rows] = w_a[m * (P // d) + e]
            out[n, rows, 1, rows] = w_x[m * (P // d) + e]
        out[n, :, 2, :] = w_pool[m]
    for m in range(DT):
        put(PANELS[("out", m)], w_out, Y_ORDER, m)
        put(PANELS[("pg", m)], w_gate, range(DT), m)
        put(PANELS[("pp", m)], w_proj, range(PLE_TILES), m)
    for c in range(CHUNKS):
        for j in range(CHUNK):
            put(PANELS[("gate", c, j)], w_up, range(DT), c * CHUNK + j)
            put(PANELS[("val", c, j)], w_up, range(DT), FF // P + c * CHUNK + j)
        for m in range(DT):
            put(PANELS[("down", c, m)], w_down, range(c * CHUNK, (c + 1) * CHUNK), m)
    return out.reshape(NP, P, PANEL)


def pack_parameters(i):
    import numpy as np

    def tiles(a):
        return np.asarray(a).reshape(-1, P).T

    ffn = np.stack([*np.asarray(i["w_conv_ffn"])[0], np.asarray(i["b_conv_ffn"])[0]])
    ffn = ffn.reshape(FFN_TAPS + 1, 2, CHUNKS, CHUNK, P).transpose(4, 2, 3, 1, 0).reshape(P, -1)
    w_lru = np.asarray(i["w_conv_lru"])[0].reshape(LRU_TAPS, GROUPS, P).transpose(2, 1, 0).reshape(P, -1)
    return np.concatenate([tiles(i["g_mix"]), tiles(i["g_ffn"]), tiles(i["g_ple"]), tiles(i["g_final"]), w_lru,
                           tiles(i["b_conv_lru"]), tiles(i["b_a"]), tiles(i["b_x"]), tiles(i["lam"]),
                           tiles(i["b_pool"]), tiles(i["pool_scale"]), tiles(i["b_ple_gate"]), ffn], axis=1)


def kernel(**inputs):
    import numpy as np
    import concourse.bacc as bacc
    from concourse.bass_utils import run_bass_kernel_spmd

    nc = bacc.Bacc("TRN2", target_bir_lowering=False, num_devices=1)
    arrays = {
        "xT": np.ascontiguousarray(np.asarray(inputs["x"])[0].T),
        "pT": np.ascontiguousarray(np.asarray(inputs["p"])[0, 0].T),
        "panels": pack_panels(inputs),
        "parameters": np.ascontiguousarray(pack_parameters(inputs)),
    }
    args = [nc.dram_tensor(n, a.shape, mybir.dt.from_np(a.dtype), kind="ExternalInput").ap()
            for n, a in arrays.items()]
    args.append(nc.dram_tensor("outT", (D, SEQ), F32, kind="ExternalOutput").ap())
    build(nc, *args)
    r = run_bass_kernel_spmd(nc, [arrays], core_ids=[0])
    return np.ascontiguousarray(r.results[0]["outT"].T)[None]
```

```python
from contextlib import ExitStack, contextmanager

import concourse.bass as bass
from concourse import mybir

F32 = mybir.dt.float32
F32R = mybir.dt.float32r
ALU = mybir.AluOpType
ACT = mybir.ActivationFunctionType

P = 128
SEQ, D = 2048, 1024
BLOCK = 1024
BLOCKS = SEQ // BLOCK
BANK = 512
HALVES = BLOCK // BANK
DT = D // P
GROUPS = 4
WINDOWS = (2, 4, 8, 16)
HALO_POOL = 16
LRU_TAPS, FFN_TAPS = 4, 3
HALO_LRU, HALO_FFN = LRU_TAPS - 1, FFN_TAPS - 1
LRU_C = 8.0
EPS = 1e-6
FF = 3 * D
PLE_TILES = 2
CHUNK = 8
CHUNKS = FF // P // CHUNK
KP = 4
PANEL = KP * P
RING = 4
WIDE = BLOCK + HALO_POOL


def plan():
    jobs, panels, ends = {}, {}, []
    used = 0

    def job(name, n_panels):
        nonlocal used
        jobs[name] = len(ends)
        panels[name] = used
        used += n_panels
        ends.append(used)

    job("stat0", 0)
    for m in range(GROUPS):
        if m != 1:
            job(("L", m), 2)
            job(("P", m), 2)
            if m == 0:
                job(("G", m), 2)
        else:
            job(("P", m), 2)
        between = ("G", m) if m else ("L", 1)
        job(("a", m), 0)
        job(("x", m), 0)
        job(between, 0)
        job(("pool", m), 3)
        panels[between] = panels[("pool", m)] + 1
    for m in range(DT):
        job(("out", m), 2)
    job("stat1", 0)
    for c in range(CHUNKS):
        for j in range(CHUNK):
            job(("gate", c, j), 2)
            job(("val", c, j), 2)
        for m in range(DT):
            job(("down", c, m), 2)
    for m in range(DT):
        job(("pg", m), 2)
        if m == 0:
            job("stat2", 0)
        job(("pp", m), 1)
    job("stat3", 0)
    return jobs, panels, ends


JOBS, PANELS, ENDS = plan()
NJ, NP = len(ENDS), ENDS[-1]
CJ, CP = 3 * CHUNK, 6 * CHUNK
assert NJ % RING == 0 and NP % RING == 0 and CJ % RING == 0 and CP % RING == 0
POOL_ORDER = (0, 2, 3, 1)
Y_ORDER = [t for m in range(GROUPS) for t in (GROUPS + POOL_ORDER[m], m)]

COLS = {}


def _cols():
    at = 0
    for name, n in (("g_mix", DT), ("g_ffn", DT), ("g_ple", DT), ("g_final", DT), ("w_lru", LRU_TAPS * GROUPS),
                    ("b_lru", GROUPS), ("b_a", GROUPS), ("b_x", GROUPS), ("lam", GROUPS), ("b_pool", GROUPS),
                    ("pool_scale", GROUPS), ("b_gate", DT), ("ffn", CHUNKS * CHUNK * 2 * (FFN_TAPS + 1))):
        COLS[name] = at
        at += n
    return at


NPAR = _cols()
CHUNK_PAR = CHUNK * 2 * (FFN_TAPS + 1)
X_SQUARES = {3: range(0, 3), 4: range(3, 6), 5: range(6, 8)}
U_BLOCK = (CHUNKS + 2) * DT


class Chain:

    def __init__(self, eng, sem, per_block):
        self.eng, self.sem, self.per_block = eng, sem, per_block
        self.base, self.k = 0, 0

    def mark(self, ins):
        ins.then_inc(self.sem, 1)
        self.k += 1
        return self.base + self.k

    def link(self, ins):
        self.eng.wait_ge(self.sem, self.mark(ins))

    def block(self, b, before):
        self.base, self.k = b * self.per_block + before, 0

    def end(self):
        assert self.k == self.per_block, ("chain per block", self.k)

    @contextmanager
    def loop(self, c, n, per_iter):
        base, k = self.base, self.k
        self.base = base + c * per_iter
        yield
        assert self.k - k == per_iter, ("chain per iteration", self.k - k)
        self.base, self.k = base, k + n * per_iter


def build(nc, xT, pT, wpan, par_d, outT):
    with ExitStack() as ctx:
        def sb(name, shape, dt=F32):
            return ctx.enter_context(nc.sbuf_tensor(name, shape, dt))

        def sem(name):
            return ctx.enter_context(nc.semaphore(name))

        H = sb("H", [P, DT, BLOCK])
        Uhi = sb("Uhi", [P, DT, BLOCK], F32R)
        Ulo = sb("Ulo", [P, DT, BLOCK], F32R)
        Y_A = sb("Y_A", [P, DT // 2, BLOCK], F32R)
        with nc.sbuf_tensor("XQ", [P, DT // 2, BLOCK], F32) as XQ:
            pass
        Y_B = sb("Y_B", [P, DT // 2, BLOCK], F32R)
        with nc.sbuf_tensor("XN", [P, DT, BLOCK], F32) as XN:
            pass
        Ylo = sb("Ylo", [P, DT, BLOCK], F32R)
        WG = sb("WG", [P, WIDE])
        WV = sb("WV", [P, WIDE])
        AG = sb("AG", [P, WIDE])
        AV = sb("AV", [P, WIDE])
        RS = sb("RS", [P, BLOCK])
        raw = [sb(f"raw{i}", [P, PANEL]) for i in range(RING)]
        whi = [sb(f"whi{i}", [P, PANEL], F32R) for i in range(RING)]
        wlo = [sb(f"wlo{i}", [P, PANEL], F32R) for i in range(RING)]
        par = sb("par", [P, NPAR])
        cpar_act = sb("cpar_act", [P, CHUNK_PAR])
        cpar_dve = sb("cpar_dve", [P, CHUNK_PAR])
        halo_ffn = sb("halo_ffn", [P, CHUNKS, CHUNK * 2 * HALO_FFN])
        halo_c = sb("halo_c", [P, CHUNK * 2 * HALO_FFN])
        halo_lru = sb("halo_lru", [P, GROUPS * HALO_LRU])
        halo_pool = sb("halo_pool", [P, GROUPS * HALO_POOL])
        ratio = sb("ratio", [P, GROUPS * HALO_POOL])
        state = sb("state", [P, GROUPS])
        means = sb("means", [P, P])
        eps_t = sb("eps_t", [P, 1])
        table_first = sb("table_first", [P, 4])
        decay = sb("decay", [P, GROUPS])
        ndecay = sb("ndecay", [P, GROUPS])
        pbs = sb("pbs", [P, GROUPS])
        sp = sb("sp", [P, 5 * GROUPS])

        slot = [ctx.enter_context(nc.psum_tensor(f"slot{i}", [P, BLOCK], F32)) for i in range(RING)]

        G, PO, R, I, S, T = (H[:, k, :] for k in range(6))
        X_tiles = [XQ[:, 2, :]] + [H[:, 6, :]] * (GROUPS - 1)

        def yhi(k):
            return (Y_A if k < DT // 2 else Y_B)[:, k % (DT // 2), :]

        par_in = sem("par_in")
        x_in = [sem(f"x_in{i}") for i in range(4)]
        x_again = [sem(f"x_again{i}") for i in range(4)]
        p_in = sem("p_in")
        panel_in = [sem(f"panel_in{i}") for i in range(RING)]
        panel_hi, panel_lo = sem("panel_hi"), sem("panel_lo")
        jobs_done = sem("jobs_done")
        slot_free = [sem(f"slot_free{i}") for i in range(RING)]
        zeroed = sem("zeroed")
        u_hi, u_ready = sem("u_hi"), sem("u_ready")
        sq_ready, ss_added = sem("sq_ready"), sem("ss_added")
        xsq_ready, xss_added = sem("xsq_ready"), sem("xss_added")
        ln_ready, rms_ready = sem("ln_ready"), sem("rms_ready")
        zl_ready, xc_sum, xc_ready = sem("zl_ready"), sem("xc_sum"), sem("xc_ready")
        xh_ready, gates_in = sem("xh_ready"), sem("gates_in")
        tanh_ready, decay_ready, onemin_ready = sem("tanh_ready"), sem("decay_ready"), sem("onemin_ready")
        mult_ready, gelu_ready, asq_ready = sem("mult_ready"), sem("gelu_ready"), sem("asq_ready")
        y_raw, y_hi, y_ready = sem("y_raw"), sem("y_hi"), sem("y_ready")
        pooled_raw, pooled_hi, pool_in = sem("pooled_raw"), sem("pooled_hi"), sem("pool_in")
        ug_ready, uv_ready = sem("ug_ready"), sem("uv_ready")
        g_sum, v_sum, g_conv, g_act = sem("g_sum"), sem("v_sum"), sem("g_conv"), sem("g_act")
        f_raw, f_hi, f_ready = sem("f_raw"), sem("f_hi"), sem("f_ready")
        p_hi, p_ready = sem("p_hi"), sem("p_ready")
        sg_ready, h_done = sem("sg_ready"), sem("h_done")
        out_ready = sem("out_ready")
        out_written = [sem(f"out_written{i}") for i in range(4)]
        dve_chain, act_chain = sem("dve_chain"), sem("act_chain")
        sp_dve, sp_act = sem("sp_dve"), sem("sp_act")

        def rms_tile(n):
            return RS[:] if n < 3 else XQ[:, 1, :]

        def col(name, i):
            return par[:, COLS[name] + i:COLS[name] + i + 1]

        def taps(tile, j, stream, t):
            i = (2 * j + stream) * (FFN_TAPS + 1) + t
            return tile[:, i:i + 1]

        def job_count(b, j):
            return b * NJ + j + 1

        def free_count(b, j):
            return b * (NJ // RING) + j // RING + 1

        x_tiles = xT.rearrange("(k p) (b t) -> b p k t", p=P, t=BLOCK)
        p_tiles = pT.rearrange("(k p) (b t) -> b p k t", p=P, t=BLOCK)
        out_tiles = outT.rearrange("(k p) (b t) -> b p k t", p=P, t=BLOCK)
        panel_groups = wpan.rearrange("(g s) p c -> g s p c", s=RING)
        GROUPS_OF_PANELS = NP // RING
        AHEAD = 2

        block = ctx.enter_context(nc.Block())

        @block.sync
        def _(sync):
            def x_load(b, tile, sems):
                for q in range(4):
                    sync.dma_start(tile[:, 2 * q:2 * q + 2, :], x_tiles[b, :, 2 * q:2 * q + 2, :]
                                   ).then_inc(sems[q], 16)

            def panel_group(b, g, static_g=None):
                for s in range(RING):
                    sync.wait_ge(panel_lo, (b * GROUPS_OF_PANELS + g) * RING + (s + 1 - RING))
                    sync.dma_start(raw[s][:], panel_groups[g if static_g is None else static_g, s]
                                   ).then_inc(panel_in[s], 16)

            sync.dma_start(par[:], par_d).then_inc(par_in, 16)
            for s in range(RING):
                sync.dma_start(XN[:, 2 * s:2 * s + 2, :], x_tiles[0, :, 2 * s:2 * s + 2, :]).then_inc(x_in[s], 16)
                if s < 2:
                    for n in (2 * s, 2 * s + 1):
                        sync.dma_start(raw[n][:], panel_groups[0, n]).then_inc(panel_in[n], 16)
            for g in range(1, AHEAD):
                panel_group(0, g)
            with sync.Fori(0, BLOCKS) as b:
                mix_groups = PANELS[("out", 0)] // RING
                with sync.Fori(AHEAD, mix_groups + 1) as g:
                    panel_group(b, g)
                sync.wait_ge(y_ready, b * DT + DT)
                x_load(b, H, x_again)
                ffn_groups = PANELS[("pg", 0)] // RING
                with sync.Fori(mix_groups + 1, ffn_groups + 1) as g:
                    panel_group(b, g)
                sync.wait_ge(f_ready, b * (CHUNKS * CHUNK) + CHUNKS * CHUNK)
                for k, tile in enumerate((WG, WV)):
                    sync.dma_start(tile[:, 0:BLOCK], p_tiles[b, :, k, :]).then_inc(p_in, 16)
                with sync.If(b < BLOCKS - 1):
                    sync.wait_ge(jobs_done, job_count(b, JOBS[("down", CHUNKS - 1, DT - 1)]))
                    x_load((b + 1) % BLOCKS, XN, x_in)
                with sync.Fori(ffn_groups + 1, GROUPS_OF_PANELS) as g:
                    panel_group(b, g)
                for g in range(AHEAD):
                    panel_group(b, GROUPS_OF_PANELS + g, g)
                for q in range(4):
                    for m in (2 * q, 2 * q + 1):
                        sync.wait_ge(out_ready, b * DT + m + 1)
                        sync.dma_start(out_tiles[b, :, m, :], H[:, m, :]).then_inc(out_written[q], 16)
            for q in range(4):
                sync.wait_ge(out_written[q], (BLOCKS + 1) * 32)

        @block.gpsimd
        def _(pool):
            for q in range(4):
                pool.sem_inc(out_written[q], 32)

        @block.tensor
        def _(pe):
            def panel_products(b_panels, n, j, rhs, k0, ks, first, last, ready=None):
                ps = slot[j % RING]
                pe.wait_ge(panel_lo, b_panels + n + 1)
                for k in range(ks):
                    if ready is not None:
                        pe.wait_ge(*ready(k0 + k))
                    w = slice(k * P, (k + 1) * P)
                    hi, lo = rhs(k0 + k)
                    passes = ((whi, hi), (whi, lo), (wlo, hi))
                    for i, (stat, mov) in enumerate(passes):
                        for h in range(HALVES):
                            t = slice(h * BANK, (h + 1) * BANK)
                            mm = pe.matmul(ps[:, t], stat[n % RING][:, w], mov[:, t],
                                           start=first and k == 0 and i == 0,
                                           stop=last and k == ks - 1 and i == len(passes) - 1)
                return mm

            def projection(b, j, n, rhs, tiles, ready=None, at=0, block_jobs=None, block_panels=None):
                pe.wait_ge(slot_free[j % RING], (b * (NJ // RING) if block_jobs is None else block_jobs) + j // RING + 1)
                bp = b * NP if block_panels is None else block_panels
                for i in range(0, tiles, KP):
                    mm = panel_products(bp, n + i // KP, j, rhs, i, min(KP, tiles - i),
                                        i == 0, i + KP >= tiles, ready)
                mm.then_inc(jobs_done, 1)

            def u(k):
                return Uhi[:, k, :], Ulo[:, k, :]

            def y(k):
                return yhi(k), Ylo[:, k, :]

            def p_tile(k):
                return Y_A[:, k, :], Y_A[:, PLE_TILES + k, :]

            def stat(b, n):
                j = JOBS[f"stat{n}"]
                if n:
                    pe.wait_ge(ss_added, b * (3 * (DT - 1)) + n * (DT - 1))
                else:
                    pe.wait_ge(xss_added, (b + 1) * (DT - 1))
                pe.wait_ge(slot_free[j % RING], free_count(b, j))
                for h in range(HALVES):
                    t = slice(h * BANK, (h + 1) * BANK)
                    mm = pe.matmul(slot[j % RING][:, t], means[:], AV[:, t] if n else XQ[:, 0, t],
                                   start=True, stop=True)
                mm.then_inc(jobs_done, 1)

            def small(b, name, i, tile, m, ready):
                n, j = PANELS[("a", m)], JOBS[(name, m)]
                pe.wait_ge(panel_lo, b * NP + n + 1)
                pe.wait_ge(ready, b * GROUPS + m + 1)
                pe.wait_ge(slot_free[j % RING], free_count(b, j))
                hi, lo = y(tile)
                w = slice(i * P, (i + 1) * P)
                passes = ((whi, hi), (whi, lo), (wlo, hi))
                for q, (stat_, mov) in enumerate(passes):
                    for h in range(HALVES):
                        t = slice(h * BANK, (h + 1) * BANK)
                        mm = pe.matmul(slot[j % RING][:, t], stat_[n % RING][:, w], mov[:, t],
                                       start=q == 0, stop=q == 2)
                mm.then_inc(jobs_done, 1)

            def first_of_block(b):
                return lambda k: (u_ready, b * U_BLOCK + k + 1)

            def u_valid(b, c):
                return lambda k: (u_ready, b * U_BLOCK + (c + 1) * DT + k + 1)

            pe.wait_ge(zeroed, 1)
            with pe.Fori(0, BLOCKS) as b:
                for m in range(GROUPS):
                    if m != 1:
                        projection(b, JOBS[("L", m)], PANELS[("L", m)], u, DT, first_of_block(b) if m == 0 else None)
                    if m == 0:
                        stat(b, 0)
                    projection(b, JOBS[("P", m)], PANELS[("P", m)], u, DT)
                    if m == 0:
                        projection(b, JOBS[("G", m)], PANELS[("G", m)], u, DT)
                    small(b, "a", 0, 2 * m + 1, m, gates_in)
                    small(b, "x", 1, 2 * m + 1, m, gates_in)
                    between = ("G", m) if m else ("L", 1)
                    projection(b, JOBS[between], PANELS[between], u, DT)
                    small(b, "pool", 2, 2 * m, m, pool_in)
                for m in range(DT):
                    projection(b, JOBS[("out", m)], PANELS[("out", m)], y, DT,
                               (lambda k: (y_ready, b * DT + k + 1)) if m == 0 else None)
                first_job, first_panel = JOBS[("gate", 0, 0)], PANELS[("gate", 0, 0)]
                projection(b, first_job, first_panel, u, DT, u_valid(b, 0))
                stat(b, 1)
                with pe.Fori(0, CHUNKS) as c:
                    jb = b * (NJ // RING) + c * (CJ // RING)
                    pb = b * NP + c * CP
                    for j in range(CHUNK):
                        for name in ("gate", "val"):
                            if (name, j) != ("gate", 0):
                                projection(b, JOBS[(name, 0, j)], PANELS[(name, 0, j)], u, DT,
                                           block_jobs=jb, block_panels=pb)
                    for m in range(DT):
                        projection(b, JOBS[("down", 0, m)], PANELS[("down", 0, m)], y, CHUNK,
                                   (lambda k: (f_ready, b * (CHUNKS * CHUNK) + c * CHUNK + k + 1)) if m == 0 else None,
                                   block_jobs=jb, block_panels=pb)
                    projection(b, first_job + CJ, first_panel + CP, u, DT, u_valid(b, c + 1),
                               block_jobs=jb, block_panels=pb)
                stat(b, 2)
                for m in range(DT):
                    if m:
                        projection(b, JOBS[("pg", m)], PANELS[("pg", m)], u, DT)
                    projection(b, JOBS[("pp", m)], PANELS[("pp", m)], p_tile, PLE_TILES,
                               (lambda k: (p_ready, b * PLE_TILES + k + 1)) if m == 0 else None)
                stat(b, 3)

        @block.scalar
        def _(act):
            def split(b, first, last, after=None, base=None):
                bp, bg, bj = base or (b * NP, b * (NP // RING), b * NJ)
                if after is not None and last > first:
                    act.wait_ge(jobs_done, bj + after + 1)
                for n in range(first, last):
                    act.wait_ge(panel_in[n % RING], (bg + n // RING) * 16 + 16)
                    nc.scalar.activation(whi[n % RING][:], raw[n % RING][:], ACT.Copy).then_inc(panel_hi, 1)

            def refill(b, j, base=None):
                split(b, (ENDS[j - 1] if j else 0) + RING, ENDS[j] + RING, j, base)

            def load_table(function):
                at = (ACT.Ln, ACT.Sigmoid, ACT.Sqrt, ACT.Gelu_apprx_tanh).index(function)
                nc.scalar.activation(table_first[:, at:at + 1], eps_t[:], function)

            def norm_tile(b, n, m, g, ready):
                act.wait_ge(*ready)
                if g is not None:
                    nc.scalar.activation(Uhi[:, m, :], H[:, m, :], ACT.Copy, scale=g).then_inc(u_hi, 1)
                if m >= 2:
                    act.wait_ge(ss_added, b * (3 * (DT - 1)) + (n - 1) * (DT - 1) + m - 1)
                nc.scalar.activation((AG if m else AV)[:, 0:BLOCK], H[:, m, :], ACT.Square).then_inc(sq_ready, 1)

            def x_square(b, m):
                if m % 2 == 0:
                    act.wait_ge(x_in[m // 2], b * 16 + 16)
                if m >= 4:
                    act.wait_ge(xss_added, b * (DT - 1) + m - 3)
                nc.scalar.activation(XQ[:, (m - 1) % 3 + 1 if m else 0, :], XN[:, m, :], ACT.Square
                                     ).then_inc(xsq_ready, 1)

            def x_hi(b, m):
                if m % 2 == 0:
                    act.wait_ge(x_in[m // 2], b * 16 + 16)
                nc.scalar.activation(Uhi[:, m, :], XN[:, m, :], ACT.Copy, scale=col("g_mix", m)).then_inc(u_hi, 1)

            def rms(b, n):
                j = JOBS[f"stat{n}"]
                load_table(ACT.Ln)
                act.wait_ge(jobs_done, job_count(b, j) + (n < 2))
                r = rms_tile(n)
                nc.scalar.activation(r, slot[j % RING][:], ACT.Ln, bias=eps_t[:]).then_inc(ln_ready, 1)
                act.wait_ge(ln_ready, b * 4 + n + 1)
                nc.scalar.activation(r, r, ACT.Exp, scale=-0.5).then_inc(rms_ready, 1)

            act.wait_ge(par_in, 16)
            lam = par[:, COLS["lam"]:COLS["lam"] + GROUPS]
            nc.scalar.activation(sp[:, 0:GROUPS], lam, ACT.Abs).then_inc(sp_act, 1)
            act.wait_ge(sp_act, 1)
            nc.scalar.activation(sp[:, 0:GROUPS], sp[:, 0:GROUPS], ACT.Exp, scale=-1.0).then_inc(sp_act, 1)
            x_hi(0, 0)
            split(0, 0, 2)
            x_hi(0, 1)
            for m in range(2):
                x_square(0, m)
            x_hi(0, 2)
            split(0, 2, RING)
            x_hi(0, 3)
            for m in range(2, 4):
                x_square(0, m)
            for m in range(4, DT):
                x_hi(0, m)
                x_square(0, m)
            act.wait_ge(zeroed, 1)
            act.wait_ge(sp_dve, 1)

            with act.Fori(0, BLOCKS) as b:
                rms(b, 0)

                for m in range(GROUPS):
                    X = X_tiles[m]
                    jl, jp, ja, jx, jg, jo = (JOBS[(n, m)] for n in ("L", "P", "a", "x", "G", "pool"))
                    refill(b, jl)
                    act.wait_ge(zl_ready, b * GROUPS + m + 1)
                    nc.scalar.activation(X, WG[:, HALO_LRU:HALO_LRU + BLOCK], ACT.Identity,
                                         bias=col("b_lru", m), scale=col("w_lru", 4 * m + 3)).then_inc(xc_sum, 1)
                    act.wait_ge(xc_ready, b * GROUPS + m + 1)
                    nc.scalar.activation(yhi(2 * m + 1), X, ACT.Copy).then_inc(xh_ready, 1)
                    refill(b, jp)
                    refill(b, jg)
                    load_table(ACT.Sigmoid)
                    if m == 0:
                        for q in range(4):
                            act.wait_ge(out_written[q], b * 32 + 32)
                    act.wait_ge(jobs_done, job_count(b, ja))
                    nc.scalar.activation(R, slot[ja % RING][:], ACT.Sigmoid, bias=col("b_a", m)
                                         ).then_inc(slot_free[ja % RING], 1)
                    act.wait_ge(jobs_done, job_count(b, jx))
                    nc.scalar.activation(I, slot[jx % RING][:], ACT.Sigmoid, bias=col("b_x", m)
                                         ).then_inc(slot_free[jx % RING], 1)
                    act.wait_ge(slot_free[ja % RING], free_count(b, ja) + 1)
                    nc.scalar.activation(S, R, ACT.Tanh, scale=decay[:, m:m + 1]).then_inc(tanh_ready, 1)
                    nc.scalar.activation(R, R, ACT.Exp, scale=ndecay[:, m:m + 1]).then_inc(decay_ready, 1)
                    act.wait_ge(decay_ready, b * GROUPS + m + 1)
                    nc.scalar.activation(T, R, ACT.Square).then_inc(asq_ready, 1)
                    act.wait_ge(pooled_raw, b * GROUPS + m + 1)
                    g = POOL_ORDER[m]
                    src = AV if g % 2 == 0 else AG
                    nc.scalar.activation(yhi(2 * m), src[:, HALO_POOL:WIDE], ACT.Copy).then_inc(pooled_hi, 1)
                    load_table(ACT.Sqrt)
                    act.wait_ge(onemin_ready, b * GROUPS + m + 1)
                    nc.scalar.activation(S, S, ACT.Sqrt).then_inc(mult_ready, 1)
                    load_table(ACT.Gelu_apprx_tanh)
                    act.wait_ge(slot_free[jg % RING], free_count(b, jg) + 1)
                    nc.scalar.activation(G, G, ACT.Gelu_apprx_tanh).then_inc(gelu_ready, 1)
                    act.wait_ge(jobs_done, job_count(b, jo))
                    nc.scalar.activation(PO, slot[jo % RING][:], ACT.Identity, bias=pbs[:, g:g + 1],
                                         scale=col("pool_scale", g)).then_inc(slot_free[jo % RING], 1)
                    refill(b, jo)
                    act.wait_ge(slot_free[jo % RING], free_count(b, jo) + 1)
                    nc.scalar.activation(yhi(2 * m), PO, ACT.Copy).then_inc(y_hi, 1)
                    act.wait_ge(y_raw, b * GROUPS + m + 1)
                    nc.scalar.activation(yhi(2 * m + 1), S, ACT.Copy).then_inc(y_hi, 1)

                for m in range(DT):
                    j = JOBS[("out", m)]
                    refill(b, j)
                    norm_tile(b, 1, m, col("g_ffn", m), (slot_free[j % RING], free_count(b, j) + 1))
                rms(b, 1)

                def chunk(c, last):
                    base = (b * NP + c * CP, b * (NP // RING) + c * (CP // RING), b * NJ + c * CJ)
                    pairs = b * (CHUNKS * CHUNK) + c * CHUNK
                    at = c * CHUNK_PAR + COLS["ffn"]
                    nc.scalar.copy(cpar_act[:], par[:, bass.ds(at, CHUNK_PAR)]).then_inc(act_chain, 1)
                    act.wait_ge(act_chain, b * CHUNKS + c + 1)
                    for j in range(CHUNK):
                        refill(b, JOBS[("gate", 0, j)], base)
                        act.wait_ge(ug_ready, pairs + j + 1)
                        nc.scalar.activation(AG[:, 0:BLOCK], WG[:, HALO_FFN:HALO_FFN + BLOCK], ACT.Identity,
                                             bias=taps(cpar_act, j, 0, 3), scale=taps(cpar_act, j, 0, 2)
                                             ).then_inc(g_sum, 1)
                        act.wait_ge(g_conv, pairs + j + 1)
                        nc.scalar.activation(AG[:, 0:BLOCK], AG[:, 0:BLOCK], ACT.Gelu_apprx_tanh).then_inc(g_act, 1)
                        refill(b, JOBS[("val", 0, j)], base)
                        act.wait_ge(uv_ready, pairs + j + 1)
                        nc.scalar.activation(AV[:, 0:BLOCK], WV[:, HALO_FFN:HALO_FFN + BLOCK], ACT.Identity,
                                             bias=taps(cpar_act, j, 1, 3), scale=taps(cpar_act, j, 1, 2)
                                             ).then_inc(v_sum, 1)
                        act.wait_ge(f_raw, pairs + j + 1)
                        nc.scalar.activation(yhi(j), AV[:, 0:BLOCK], ACT.Copy).then_inc(f_hi, 1)
                    for m in range(DT):
                        j = JOBS[("down", 0, m)]
                        refill(b, j, base)
                        if last:
                            jl = JOBS[("down", c, m)]
                            norm_tile(b, 2, m, col("g_ple", m), (slot_free[jl % RING], free_count(b, jl) + 1))

                with act.Fori(0, CHUNKS - 1) as c:
                    chunk(c, False)
                chunk(CHUNKS - 1, True)
                for k, tile in enumerate((WG, WV)):
                    if k == 0:
                        act.wait_ge(jobs_done, job_count(b, JOBS[("down", CHUNKS - 1, DT - 1)]))
                        act.wait_ge(p_in, b * 32 + 32)
                    nc.scalar.activation(yhi(k), tile[:, 0:BLOCK], ACT.Copy).then_inc(p_hi, 1)
                rms(b, 2)
                for m in range(DT):
                    jg, jp = JOBS[("pg", m)], JOBS[("pp", m)]
                    refill(b, jg)
                    act.wait_ge(slot_free[jg % RING], free_count(b, jg) + 1)
                    nc.scalar.activation(WG[:, 0:BLOCK], WG[:, 0:BLOCK], ACT.Sigmoid, bias=col("b_gate", m)
                                         ).then_inc(sg_ready, 1)
                    refill(b, jp)
                    norm_tile(b, 3, m, None, (h_done, b * DT + m + 1))
                    if m in X_SQUARES:
                        with act.If(b < BLOCKS - 1):
                            for k in X_SQUARES[m]:
                                x_square(b + 1, k)
                with act.If(b < BLOCKS - 1):
                    for m in range(DT // 2):
                        x_hi(b + 1, m)
                rms(b, 3)
                with act.If(b < BLOCKS - 1):
                    for m in range(DT // 2, DT):
                        x_hi(b + 1, m)

        @block.vector
        def _(dve):
            v = nc.vector
            chain = Chain(dve, dve_chain, DVE_PER_BLOCK)

            def f32(ap):
                return ap.bitcast(F32)

            def split(first, last, bp):
                for n in range(first, last):
                    dve.wait_ge(panel_hi, bp + n + 1)
                    v.tensor_tensor(wlo[n % RING][:], raw[n % RING][:], f32(whi[n % RING][:]), ALU.subtract
                                    ).then_inc(panel_lo, 1)

            def refill(j, bp):
                split((ENDS[j - 1] if j else 0) + RING, ENDS[j] + RING, bp)

            def scaled_out(b, j, dst, bj=None, bs=None):
                dve.wait_ge(jobs_done, (b * NJ if bj is None else bj) + j + 1)
                v.tensor_tensor(dst, slot[j % RING][:], RS[:], ALU.mult).then_inc(slot_free[j % RING], 1)
                dve.wait_ge(slot_free[j % RING], (b * (NJ // RING) if bs is None else bs) + j // RING + 2)

            def norm_tile(b, n, m, g):
                if g is not None:
                    dve.wait_ge(u_hi, b * (3 * DT) + n * DT + m + 1)
                    v.scalar_tensor_tensor(Ulo[:, m, :], H[:, m, :], g, f32(Uhi[:, m, :]), ALU.mult, ALU.subtract
                                           ).then_inc(u_ready, 1)
                if m:
                    dve.wait_ge(sq_ready, b * (3 * DT) + (n - 1) * DT + m + 1)
                    if m >= 2:
                        dve.wait_ge(ss_added, b * (3 * (DT - 1)) + (n - 1) * (DT - 1) + m - 1)
                    v.tensor_tensor(AV[:, 0:BLOCK], AV[:, 0:BLOCK], AG[:, 0:BLOCK], ALU.add).then_inc(ss_added, 1)

            def x_sum(b, m):
                dve.wait_ge(xsq_ready, b * DT + m + 1)
                if m >= 2:
                    dve.wait_ge(xss_added, b * (DT - 1) + m - 1)
                v.tensor_tensor(XQ[:, 0, :], XQ[:, 0, :], XQ[:, (m - 1) % 3 + 1, :], ALU.add).then_inc(xss_added, 1)

            def x_lo(b, m):
                dve.wait_ge(u_hi, b * (3 * DT) + m + 1)
                v.scalar_tensor_tensor(Ulo[:, m, :], XN[:, m, :], col("g_mix", m), f32(Uhi[:, m, :]),
                                       ALU.mult, ALU.subtract).then_inc(u_ready, 1)

            def rstd(b, n):
                j = JOBS[f"stat{n}"]
                t = AV[:, 0:BLOCK]
                dve.wait_ge(rms_ready, b * 4 + n + 1)
                r = rms_tile(n)
                v.scalar_tensor_tensor(t, slot[j % RING][:], eps_t[:], r, ALU.add, ALU.mult
                                       ).then_inc(slot_free[j % RING], 1)
                dve.wait_ge(slot_free[j % RING], free_count(b, j) + 1)
                chain.link(v.scalar_tensor_tensor(t, t, -0.5, r, ALU.mult, ALU.mult))
                return chain.mark(v.scalar_tensor_tensor(r, t, 1.5, r, ALU.add, ALU.mult))

            chain.link(v.memset(means[:], 1.0 / D))
            chain.link(v.memset(eps_t[:], EPS))
            chain.link(v.memset(halo_ffn[:], 0.0))
            chain.link(v.memset(halo_lru[:], 0.0))
            chain.link(v.memset(halo_pool[:], 0.0))
            chain.link(v.memset(state[:], 0.0))
            dve.sem_inc(zeroed, 1)
            for s in range(RING):
                dve.sem_inc(slot_free[s], 1)
            x_lo(0, 0)
            split(0, 2, 0)
            x_lo(0, 1)
            x_sum(0, 1)
            e, z, z2, q, neg = (sp[:, i * GROUPS:(i + 1) * GROUPS] for i in range(5))
            lam = par[:, COLS["lam"]:COLS["lam"] + GROUPS]
            dve.wait_ge(zeroed, 1)
            dve.wait_ge(sp_act, 2)
            chain.link(v.tensor_scalar(z, e, 2.0, None, ALU.add))
            chain.link(v.reciprocal(z, z))
            chain.link(v.tensor_tensor(z, z, e, ALU.mult))
            chain.link(v.tensor_tensor(z2, z, z, ALU.mult))
            chain.link(v.tensor_scalar(q, z2, 1.0 / 17, None, ALU.mult))
            for d in (15, 13, 11, 9, 7, 5, 3):
                chain.link(v.scalar_tensor_tensor(q, q, 1.0 / d, z2, ALU.add, ALU.mult))
            chain.link(v.scalar_tensor_tensor(q, q, 1.0, z, ALU.add, ALU.mult))
            chain.link(v.tensor_scalar(q, q, 2.0, None, ALU.mult))
            chain.link(v.tensor_scalar(neg, lam, -1.0, 0.0, ALU.mult, ALU.max))
            chain.link(v.tensor_tensor(q, q, neg, ALU.add))
            chain.link(v.tensor_scalar(decay[:], q, LRU_C, None, ALU.mult))
            chain.link(v.tensor_scalar(ndecay[:], q, -LRU_C, None, ALU.mult))
            v.tensor_tensor(pbs[:], par[:, COLS["b_pool"]:COLS["b_pool"] + GROUPS],
                            par[:, COLS["pool_scale"]:COLS["pool_scale"] + GROUPS], ALU.mult).then_inc(sp_dve, 1)
            x_lo(0, 2)
            split(2, RING, 0)
            x_lo(0, 3)
            for m in range(2, 4):
                x_sum(0, m)
            for m in range(4, DT):
                x_lo(0, m)
                x_sum(0, m)
            chain.link(v.memset(ratio[:], 1.0))
            for g, w in enumerate(WINDOWS):
                for t in range(w - 1):
                    chain.link(v.memset(ratio[:, g * HALO_POOL + t:g * HALO_POOL + t + 1], w / (t + 1.0)))
            before = chain.k

            def outputs():
                for m in range(DT):
                    v.scalar_tensor_tensor(H[:, m, :], H[:, m, :], col("g_final", m), rms_tile(3), ALU.mult, ALU.mult
                                           ).then_inc(out_ready, 1)

            with dve.Fori(0, BLOCKS) as b:
                chain.block(b, before)
                bp = b * NP
                dve.wait_ge(dve_chain, rstd(b, 0))

                for m in range(GROUPS):
                    X = X_tiles[m]
                    jl, jp, ja, jx, jg, jo = (JOBS[(n, m)] for n in ("L", "P", "a", "x", "G", "pool"))
                    halo = halo_lru[:, m * HALO_LRU:(m + 1) * HALO_LRU]
                    v.tensor_copy(WG[:, 0:HALO_LRU], halo)
                    scaled_out(b, jl, WG[:, HALO_LRU:HALO_LRU + BLOCK])
                    v.tensor_copy(halo, WG[:, BLOCK:BLOCK + HALO_LRU]).then_inc(zl_ready, 1)
                    refill(jl, bp)
                    dve.wait_ge(xc_sum, b * GROUPS + m + 1)
                    for t in (2, 1, 0):
                        tap = v.scalar_tensor_tensor(X, WG[:, t:t + BLOCK], col("w_lru", 4 * m + t), X,
                                                     ALU.mult, ALU.add)
                        if t:
                            chain.link(tap)
                        else:
                            tap.then_inc(xc_ready, 1)
                    dve.wait_ge(xh_ready, b * GROUPS + m + 1)
                    v.tensor_tensor(Ylo[:, 2 * m + 1, :], X, f32(yhi(2 * m + 1)), ALU.subtract
                                    ).then_inc(gates_in, 1)
                    g = POOL_ORDER[m]
                    halo = halo_pool[:, g * HALO_POOL:(g + 1) * HALO_POOL]
                    v.tensor_copy(WV[:, 0:HALO_POOL], halo)
                    scaled_out(b, jp, WV[:, HALO_POOL:WIDE])
                    chain.link(v.tensor_copy(halo, WV[:, BLOCK:WIDE]))
                    refill(jp, bp)
                    if m == 0:
                        with dve.If(b > 0):
                            outputs()
                    refill(jg, bp)
                    src, dst, w = WV, AG, 1
                    while w < WINDOWS[g]:
                        chain.link(v.tensor_tensor(dst[:, 2 * w:WIDE], src[:, 2 * w:WIDE], src[:, w:WIDE - w], ALU.add))
                        src, dst, w = dst, (AV if dst is AG else AG), 2 * w
                    chain.link(v.tensor_tensor(src[:, HALO_POOL:2 * HALO_POOL], src[:, HALO_POOL:2 * HALO_POOL],
                                               ratio[:, g * HALO_POOL:(g + 1) * HALO_POOL], ALU.mult))
                    v.scalar_tensor_tensor(dst[:, HALO_POOL:WIDE], src[:, HALO_POOL:WIDE], 1.0 / w,
                                           WV[:, HALO_POOL:WIDE], ALU.mult, ALU.subtract).then_inc(pooled_raw, 1)
                    if m == 0:
                        dve.wait_ge(out_written[0], b * 32 + 32)
                        scaled_out(b, jg, G)
                    dve.wait_ge(slot_free[jx % RING], free_count(b, jx) + 1)
                    input_gated = chain.mark(v.tensor_tensor(I, I, X, ALU.mult))
                    dve.wait_ge(tanh_ready, b * GROUPS + m + 1)
                    dve.wait_ge(asq_ready, b * GROUPS + m + 1)
                    v.scalar_tensor_tensor(S, T, 1.0, S, ALU.add, ALU.mult).then_inc(onemin_ready, 1)
                    dve.wait_ge(pooled_hi, b * GROUPS + m + 1)
                    v.tensor_tensor(Ylo[:, 2 * m, :], dst[:, HALO_POOL:WIDE], f32(yhi(2 * m)), ALU.subtract
                                    ).then_inc(pool_in, 1)
                    dve.wait_ge(dve_chain, input_gated)
                    dve.wait_ge(mult_ready, b * GROUPS + m + 1)
                    chain.link(v.tensor_tensor(I, I, S, ALU.mult))
                    dve.wait_ge(decay_ready, b * GROUPS + m + 1)
                    chain.link(v.tensor_tensor_scan(S, R, I, state[:, m:m + 1], ALU.mult, ALU.add))
                    chain.link(v.tensor_copy(state[:, m:m + 1], S[:, BLOCK - 1:BLOCK]))
                    if m:
                        scaled_out(b, jg, G)
                    dve.wait_ge(gelu_ready, b * GROUPS + m + 1)
                    v.tensor_tensor(S, S, G, ALU.mult).then_inc(y_raw, 1)
                    refill(jo, bp)
                    dve.wait_ge(y_hi, b * DT + 2 * m + 1)
                    v.tensor_tensor(Ylo[:, 2 * m, :], PO, f32(yhi(2 * m)), ALU.subtract).then_inc(y_ready, 1)
                    dve.wait_ge(y_hi, b * DT + 2 * m + 2)
                    v.tensor_tensor(Ylo[:, 2 * m + 1, :], S, f32(yhi(2 * m + 1)), ALU.subtract
                                    ).then_inc(y_ready, 1)
                v.memset(ratio[:], 1.0)

                for m in range(DT):
                    j = JOBS[("out", m)]
                    dve.wait_ge(jobs_done, job_count(b, j))
                    if m % 2 == 0:
                        dve.wait_ge(x_again[m // 2], b * 16 + 16)
                    v.tensor_tensor(H[:, m, :], slot[j % RING][:], H[:, m, :], ALU.add
                                    ).then_inc(slot_free[j % RING], 1)
                    refill(j, bp)
                    norm_tile(b, 1, m, col("g_ffn", m))
                ffn_scale = rstd(b, 1)

                def chunk(c, last):
                    bp_c, bj, bs = b * NP + c * CP, b * NJ + c * CJ, b * (NJ // RING) + c * (CJ // RING)
                    pairs = b * (CHUNKS * CHUNK) + c * CHUNK
                    v.tensor_copy(cpar_dve[:], par[:, bass.ds(c * CHUNK_PAR + COLS["ffn"], CHUNK_PAR)])
                    chain.link(v.tensor_copy(halo_c[:], halo_ffn[:, bass.ds(c, 1), :]))

                    def f_lo(j):
                        dve.wait_ge(f_hi, pairs + j + 1)
                        v.tensor_tensor(Ylo[:, j, :], AV[:, 0:BLOCK], f32(yhi(j)), ALU.subtract
                                        ).then_inc(f_ready, 1)

                    def conv(j, stream, work, acc, ready, summed):
                        jj = JOBS[(("gate", "val")[stream], 0, j)]
                        i = (2 * j + stream) * HALO_FFN
                        v.tensor_copy(work[:, 0:HALO_FFN], halo_c[:, i:i + HALO_FFN])
                        if (j, stream) == (0, 0):
                            dve.wait_ge(dve_chain, ffn_scale)
                        scaled_out(b, jj, work[:, HALO_FFN:HALO_FFN + BLOCK], bj, bs)
                        if stream == 0 and j:
                            f_lo(j - 1)
                        v.tensor_copy(halo_c[:, i:i + HALO_FFN], work[:, BLOCK:BLOCK + HALO_FFN]).then_inc(ready, 1)
                        refill(jj, bp_c)
                        dve.wait_ge(summed, pairs + j + 1)
                        chain.link(v.scalar_tensor_tensor(acc[:, 0:BLOCK], work[:, 1:1 + BLOCK],
                                                          taps(cpar_dve, j, stream, 1), acc[:, 0:BLOCK],
                                                          ALU.mult, ALU.add))
                        return v.scalar_tensor_tensor(acc[:, 0:BLOCK], work[:, 0:BLOCK],
                                                      taps(cpar_dve, j, stream, 0), acc[:, 0:BLOCK],
                                                      ALU.mult, ALU.add)

                    for j in range(CHUNK):
                        conv(j, 0, WG, AG, ug_ready, g_sum).then_inc(g_conv, 1)
                        chain.link(conv(j, 1, WV, AV, uv_ready, v_sum))
                        dve.wait_ge(g_act, pairs + j + 1)
                        v.tensor_tensor(AV[:, 0:BLOCK], AG[:, 0:BLOCK], AV[:, 0:BLOCK], ALU.mult).then_inc(f_raw, 1)
                    f_lo(CHUNK - 1)
                    v.tensor_copy(halo_ffn[:, bass.ds(c, 1), :], halo_c[:])
                    for m in range(DT):
                        jj = JOBS[("down", 0, m)]
                        dve.wait_ge(jobs_done, bj + jj + 1)
                        v.tensor_tensor(H[:, m, :], slot[jj % RING][:], H[:, m, :], ALU.add
                                        ).then_inc(slot_free[jj % RING], 1)
                        refill(jj, bp_c)
                        if last:
                            norm_tile(b, 2, m, col("g_ple", m))
                        elif m == 0:
                            dve.sem_inc(u_ready, DT)

                with dve.Fori(0, CHUNKS - 1) as c, chain.loop(c, CHUNKS - 1, DVE_PER_CHUNK):
                    chunk(c, False)
                chunk(CHUNKS - 1, True)
                for k, tile in enumerate((WG, WV)):
                    dve.wait_ge(p_hi, b * PLE_TILES + k + 1)
                    v.tensor_tensor(yhi(PLE_TILES + k), tile[:, 0:BLOCK], f32(yhi(k)), ALU.subtract
                                    ).then_inc(p_ready, 1)
                dve.wait_ge(dve_chain, rstd(b, 2))
                for m in range(DT):
                    jg, jp = JOBS[("pg", m)], JOBS[("pp", m)]
                    scaled_out(b, jg, WG[:, 0:BLOCK])
                    refill(jg, bp)
                    dve.wait_ge(sg_ready, b * DT + m + 1)
                    dve.wait_ge(jobs_done, job_count(b, jp))
                    v.tensor_tensor(WV[:, 0:BLOCK], slot[jp % RING][:], WG[:, 0:BLOCK], ALU.mult
                                    ).then_inc(slot_free[jp % RING], 1)
                    refill(jp, bp)
                    dve.wait_ge(slot_free[jp % RING], free_count(b, jp) + 1)
                    v.tensor_tensor(H[:, m, :], H[:, m, :], WV[:, 0:BLOCK], ALU.add).then_inc(h_done, 1)
                    norm_tile(b, 3, m, None)
                    if m in X_SQUARES:
                        with dve.If(b < BLOCKS - 1):
                            for k in X_SQUARES[m]:
                                if k:
                                    x_sum(b + 1, k)
                with dve.If(b < BLOCKS - 1):
                    for m in range(DT):
                        x_lo(b + 1, m)
                dve.wait_ge(dve_chain, rstd(b, 3))
                chain.end()
            outputs()


DVE_PER_BLOCK = 125
DVE_PER_CHUNK = 25


def pack_panels(i):
    import numpy as np
    w_in, w_out, w_up, w_down, w_gate, w_proj = (
        np.asarray(i[n])[0].reshape(-1, P, np.asarray(i[n]).shape[-1])
        for n in ("w_in", "w_out", "w_up", "w_down", "w_ple_gate", "w_ple_proj"))
    w_a, w_x, w_pool = (np.asarray(i[n])[0] for n in ("w_a", "w_x", "w_pool"))
    out = np.zeros((NP, P, KP, P), w_in.dtype)

    def put(first, w, tiles, m):
        for n, k in enumerate(tiles):
            out[first + n // KP, :, n % KP, :] = w[k, :, m * P:(m + 1) * P]

    for m in range(GROUPS):
        for s, name in enumerate(("L", "G", "P")):
            put(PANELS[(name, m)], w_in, range(DT), s * GROUPS + (POOL_ORDER[m] if name == "P" else m))
        n = PANELS[("pool", m)]
        d = w_a.shape[-1]
        for e in range(P // d):
            rows = slice(e * d, (e + 1) * d)
            out[n, rows, 0, rows] = w_a[m * (P // d) + e]
            out[n, rows, 1, rows] = w_x[m * (P // d) + e]
        out[n, :, 2, :] = w_pool[POOL_ORDER[m]]
    for m in range(DT):
        put(PANELS[("out", m)], w_out, Y_ORDER, m)
        put(PANELS[("pg", m)], w_gate, range(DT), m)
        put(PANELS[("pp", m)], w_proj, range(PLE_TILES), m)
    for c in range(CHUNKS):
        for j in range(CHUNK):
            put(PANELS[("gate", c, j)], w_up, range(DT), c * CHUNK + j)
            put(PANELS[("val", c, j)], w_up, range(DT), FF // P + c * CHUNK + j)
        for m in range(DT):
            put(PANELS[("down", c, m)], w_down, range(c * CHUNK, (c + 1) * CHUNK), m)
    return out.reshape(NP, P, PANEL)


def pack_parameters(i):
    import numpy as np

    def tiles(a):
        return np.asarray(a).reshape(-1, P).T

    ffn = np.stack([*np.asarray(i["w_conv_ffn"])[0], np.asarray(i["b_conv_ffn"])[0]])
    ffn = ffn.reshape(FFN_TAPS + 1, 2, CHUNKS, CHUNK, P).transpose(4, 2, 3, 1, 0).reshape(P, -1)
    w_lru = np.asarray(i["w_conv_lru"])[0].reshape(LRU_TAPS, GROUPS, P).transpose(2, 1, 0).reshape(P, -1)
    return np.concatenate([tiles(i["g_mix"]), tiles(i["g_ffn"]), tiles(i["g_ple"]), tiles(i["g_final"]), w_lru,
                           tiles(i["b_conv_lru"]), tiles(i["b_a"]), tiles(i["b_x"]), tiles(i["lam"]),
                           tiles(i["b_pool"]), tiles(i["pool_scale"]), tiles(i["b_ple_gate"]), ffn], axis=1)


def kernel(**inputs):
    import numpy as np
    import concourse.bacc as bacc
    from concourse.bass_utils import run_bass_kernel_spmd

    nc = bacc.Bacc("TRN2", target_bir_lowering=False, num_devices=1)
    arrays = {
        "xT": np.ascontiguousarray(np.asarray(inputs["x"])[0].T),
        "pT": np.ascontiguousarray(np.asarray(inputs["p"])[0, 0].T),
        "panels": pack_panels(inputs),
        "parameters": np.ascontiguousarray(pack_parameters(inputs)),
    }
    args = [nc.dram_tensor(n, a.shape, mybir.dt.from_np(a.dtype), kind="ExternalInput").ap()
            for n, a in arrays.items()]
    args.append(nc.dram_tensor("outT", (D, SEQ), F32, kind="ExternalOutput").ap())
    build(nc, *args)
    r = run_bass_kernel_spmd(nc, [arrays], core_ids=[0])
    return np.ascontiguousarray(r.results[0]["outT"].T)[None]
```
